# Optimizing a Trainium2 kernel written in Bass

```python
import jax, jax.numpy as jnp
from jax import lax
import numpy as np

D_MODEL = 1024
BATCH = 1
SEQ = 512
DEPTH = 1

HEAD_DIM = 64
FOX_HEADS = 6
FOX_WIDTH = FOX_HEADS * HEAD_DIM
POOL_GROUPS = 4
POOL_GROUP_DIM = 64
POOL_WINDOWS = (2, 4, 8, 16)
POOL_WIDTH = POOL_GROUPS * POOL_GROUP_DIM
NSA_HEADS = 6
NSA_KV_HEADS = 2
NSA_REP = NSA_HEADS // NSA_KV_HEADS
NSA_WIDTH = NSA_HEADS * HEAD_DIM
KV_WIDTH = NSA_KV_HEADS * HEAD_DIM
N_BRANCH = 3
CMP_LEN = 32
CMP_STRIDE = 16
CMP_HIDDEN = 256
SEL_BLOCK = 64
SEL_TOPN = 16
WINDOW = 512
FORCE_SCORE = 1.0e4
Q_BLOCK = 128
MIX_WIDTH = FOX_WIDTH + POOL_WIDTH + NSA_WIDTH
IN_SPLITS = (FOX_WIDTH, FOX_WIDTH, FOX_WIDTH, FOX_HEADS, POOL_WIDTH, NSA_WIDTH,
             KV_WIDTH, KV_WIDTH, KV_WIDTH, KV_WIDTH, KV_WIDTH, KV_WIDTH, NSA_HEADS * N_BRANCH)
IN_WIDTH = 3 * FOX_WIDTH + FOX_HEADS + POOL_WIDTH + NSA_WIDTH + 6 * KV_WIDTH + NSA_HEADS * N_BRANCH
MEM_LEN = 256
MEM_HEADS = 4
MEM_HEAD_DIM = D_MODEL // MEM_HEADS
N_GROUPS = 4
EXPERTS_PER_GROUP = 4
N_EXPERTS = N_GROUPS * EXPERTS_PER_GROUP
FINE_TOP_K = 2
EXPERT_FF = 512

EPS = 1e-6
NEG_INF = -1e30

kernel_name = "hybrid_fox_pool_nsa_hmoe"

def _split_points():
    pts, acc = [], 0
    for s in IN_SPLITS[:-1]:
        acc += s
        pts.append(acc)
    return pts

def rms_norm(x, g):
    xf = x.astype(jnp.float32)
    y = xf * lax.rsqrt(jnp.mean(xf * xf, axis=-1, keepdims=True) + EPS)
    return (y * g.astype(jnp.float32)).astype(x.dtype)

def masked_softmax(s, valid):
    p = jax.nn.softmax(jnp.where(valid, s, NEG_INF), axis=-1)
    return jnp.where(valid, p, 0.0)

def alibi_slopes(n_heads):
    return jnp.exp2(-8.0 * jnp.arange(1, n_heads + 1, dtype=jnp.float32) / n_heads)

def fox_attention(q, k, v, f_logit, b_f):
    bsz, T, _ = q.shape
    H, dh = FOX_HEADS, HEAD_DIM
    heads = lambda t: t.reshape(bsz, T, H, dh).transpose(0, 2, 1, 3)
    q, k, v = heads(q), heads(k), heads(v)
    log_f = jax.nn.log_sigmoid(f_logit.astype(jnp.float32) + b_f.astype(jnp.float32))
    cum = jnp.cumsum(log_f, axis=1).transpose(0, 2, 1)
    scale = dh ** -0.5
    kpos = jnp.arange(T)

    def block(i):
        q0 = i * Q_BLOCK
        qb = lax.dynamic_slice_in_dim(q, q0, Q_BLOCK, axis=2)
        cq = lax.dynamic_slice_in_dim(cum, q0, Q_BLOCK, axis=2)
        s = (jnp.einsum('bhqd,bhkd->bhqk', qb, k).astype(jnp.float32) * scale
             + cq[..., :, None] - cum[:, :, None, :])
        qpos = q0 + jnp.arange(Q_BLOCK)
        p = masked_softmax(s, kpos[None, :] <= qpos[:, None])
        return jnp.einsum('bhqk,bhkd->bhqd', p.astype(v.dtype), v)

    out = lax.map(block, jnp.arange(T // Q_BLOCK))
    return out.transpose(1, 0, 3, 2, 4).reshape(bsz, T, H * dh)

def pool_mixer(u, w_pool, scale):
    bsz, T, _ = u.shape
    uf = u.astype(jnp.float32).reshape(bsz, T, POOL_GROUPS, POOL_GROUP_DIM)
    cs = jnp.concatenate([jnp.zeros((bsz, 1, POOL_GROUPS, POOL_GROUP_DIM), jnp.float32),
                          jnp.cumsum(uf, axis=1)], axis=1)
    t = jnp.arange(T)
    outs = []
    for gi, w in enumerate(POOL_WINDOWS):
        start = jnp.maximum(t + 1 - w, 0)
        win_sum = cs[:, 1:, gi] - cs[:, start, gi]
        count = jnp.minimum(t + 1, w).astype(jnp.float32)
        outs.append(win_sum / count[None, :, None] - uf[:, :, gi])
    pooled = jnp.stack(outs, axis=2).astype(u.dtype)
    mixed = jnp.einsum('btgc,gcd->btgd', pooled, w_pool)
    return mixed.reshape(bsz, T, POOL_WIDTH) * scale

def nsa_attention(q, k_cmp, v_cmp, k_slc, v_slc, k_win, v_win, gate_logit, gate_b,
                  pe_k, pe_v, w1_k, w2_k, w1_v, w2_v):
    bsz, T, _ = q.shape
    G, R, dh = NSA_KV_HEADS, NSA_REP, HEAD_DIM
    scale = dh ** -0.5
    qh = q.reshape(bsz, T, G, R, dh).transpose(0, 2, 3, 1, 4)
    kv_heads = lambda t: t.reshape(bsz, T, G, dh).transpose(0, 2, 1, 3)
    k_cmp, v_cmp, k_slc, v_slc, k_win, v_win = (kv_heads(t) for t in (k_cmp, v_cmp, k_slc, v_slc, k_win, v_win))
    gates = jax.nn.sigmoid(gate_logit.astype(jnp.float32) + gate_b.astype(jnp.float32))
    gates = gates.reshape(bsz, T, G, R, N_BRANCH).transpose(0, 2, 3, 1, 4)

    n_chunk = T // CMP_STRIDE
    n_sub = CMP_LEN // CMP_STRIDE
    n_cmp = n_chunk - n_sub + 1

    def compress(t, pe, w1, w2):
        ch = t.reshape(bsz, G, n_chunk, CMP_STRIDE, dh)
        blocks = jnp.concatenate([ch[:, :, j:j + n_cmp] for j in range(n_sub)], axis=3)
        flat = (blocks + pe).reshape(bsz, G, n_cmp, CMP_LEN * dh)
        return jax.nn.gelu(flat @ w1) @ w2

    kc = compress(k_cmp, pe_k, w1_k, w2_k)
    vc = compress(v_cmp, pe_v, w1_v, w2_v)
    c_start = jnp.arange(n_cmp) * CMP_STRIDE
    c_end = c_start + CMP_LEN - 1

    n_sel_blk = T // SEL_BLOCK
    n_top = min(SEL_TOPN, n_sel_blk)
    s_start = jnp.arange(n_sel_blk) * SEL_BLOCK
    overlap = ((c_start[:, None] < s_start[None, :] + SEL_BLOCK)
               & (c_end[:, None] >= s_start[None, :])).astype(jnp.float32)
    ks_blk = k_slc.reshape(bsz, G, n_sel_blk, SEL_BLOCK, dh)
    vs_blk = v_slc.reshape(bsz, G, n_sel_blk, SEL_BLOCK, dh)
    kw_pad = jnp.pad(k_win, ((0, 0), (0, 0), (WINDOW, 0), (0, 0)))
    vw_pad = jnp.pad(v_win, ((0, 0), (0, 0), (WINDOW, 0), (0, 0)))
    slopes = alibi_slopes(NSA_HEADS).reshape(1, G, R, 1, 1)
    b_idx = jnp.arange(bsz)[:, None, None, None]
    g_idx = jnp.arange(G)[None, :, None, None]
    blk_ids = jnp.arange(n_sel_blk)
    in_blk = jnp.arange(SEL_BLOCK)
    win_off = jnp.arange(WINDOW + Q_BLOCK)

    def block(i):
        q0 = i * Q_BLOCK
        qb = lax.dynamic_slice_in_dim(qh, q0, Q_BLOCK, axis=3)
        gb = lax.dynamic_slice_in_dim(gates, q0, Q_BLOCK, axis=3)
        tq = q0 + jnp.arange(Q_BLOCK)

        dist_c = tq[:, None] - c_end[None, :]
        s_c = (jnp.einsum('bgrqd,bgcd->bgrqc', qb, kc).astype(jnp.float32) * scale
               - slopes * dist_c.astype(jnp.float32))
        p_c = masked_softmax(s_c, dist_c >= 0)
        o_c = jnp.einsum('bgrqc,bgcd->bgrqd', p_c.astype(vc.dtype), vc)

        imp = jnp.einsum('bgrqc,cj->bgqj', p_c, overlap)
        cur = tq // SEL_BLOCK
        forced = ((blk_ids[None, :] == 0) | (blk_ids[None, :] == cur[:, None])
                  | (blk_ids[None, :] == cur[:, None] - 1))
        causal_blk = blk_ids[None, :] <= cur[:, None]
        score = jnp.where(forced, FORCE_SCORE, jnp.where(causal_blk, imp, -1.0))
        _, sel = lax.top_k(score, n_top)

        k_sel = ks_blk[b_idx, g_idx, sel].reshape(bsz, G, Q_BLOCK, n_top * SEL_BLOCK, dh)
        v_sel = vs_blk[b_idx, g_idx, sel].reshape(bsz, G, Q_BLOCK, n_top * SEL_BLOCK, dh)
        pos = (sel[..., None] * SEL_BLOCK + in_blk).reshape(bsz, G, Q_BLOCK, n_top * SEL_BLOCK)
        dist_s = (tq[None, None, :, None] - pos)[:, :, None]
        s_s = (jnp.einsum('bgrqd,bgqld->bgrql', qb, k_sel).astype(jnp.float32) * scale
               - slopes * dist_s.astype(jnp.float32))
        p_s = masked_softmax(s_s, dist_s >= 0)
        o_s = jnp.einsum('bgrql,bgqld->bgrqd', p_s.astype(v_sel.dtype), v_sel)

        kw = lax.dynamic_slice_in_dim(kw_pad, q0, WINDOW + Q_BLOCK, axis=2)
        vw = lax.dynamic_slice_in_dim(vw_pad, q0, WINDOW + Q_BLOCK, axis=2)
        pk = q0 - WINDOW + win_off
        dist_w = tq[:, None] - pk[None, :]
        valid_w = (dist_w >= 0) & (dist_w < WINDOW) & (pk[None, :] >= 0)
        s_w = (jnp.einsum('bgrqd,bgkd->bgrqk', qb, kw).astype(jnp.float32) * scale
               - slopes * dist_w.astype(jnp.float32))
        p_w = masked_softmax(s_w, valid_w)
        o_w = jnp.einsum('bgrqk,bgkd->bgrqd', p_w.astype(vw.dtype), vw)

        o = gb[..., 0:1] * o_c + gb[..., 1:2] * o_s + gb[..., 2:3] * o_w
        return o.astype(q.dtype)

    out = lax.map(block, jnp.arange(T // Q_BLOCK))
    return out.transpose(1, 0, 4, 2, 3, 5).reshape(bsz, T, NSA_WIDTH)

def memory_cross_attention(h, mem_n, wq, wk, wv, wo):
    bsz, T, _ = h.shape
    M = mem_n.shape[1]
    q = (h @ wq).reshape(bsz, T, MEM_HEADS, MEM_HEAD_DIM)
    k = (mem_n @ wk).reshape(bsz, M, MEM_HEADS, MEM_HEAD_DIM)
    v = (mem_n @ wv).reshape(bsz, M, MEM_HEADS, MEM_HEAD_DIM)
    s = jnp.einsum('bqhd,bkhd->bhqk', q, k).astype(jnp.float32) * MEM_HEAD_DIM ** -0.5
    p = jax.nn.softmax(s, axis=-1)
    o = jnp.einsum('bhqk,bkhd->bqhd', p.astype(v.dtype), v).reshape(bsz, T, D_MODEL)
    return o @ wo

def hier_moe(h, w_coarse, b_coarse, w_fine, b_fine, w_gate, w_up, w_down):
    bsz, T, D = h.shape
    ht = h.reshape(-1, D)
    n_tok = ht.shape[0]
    p_coarse = jax.nn.softmax((ht @ w_coarse).astype(jnp.float32) + b_coarse.astype(jnp.float32), axis=-1)
    grp = jnp.argmax(p_coarse, axis=-1)
    w_grp = jnp.take_along_axis(p_coarse, grp[:, None], axis=-1)
    fine = ((ht @ w_fine).astype(jnp.float32) + b_fine.astype(jnp.float32)).reshape(n_tok, N_GROUPS, EXPERTS_PER_GROUP)
    fine = jnp.take_along_axis(fine, grp[:, None, None], axis=1)[:, 0]
    top_p, top_i = lax.top_k(jax.nn.softmax(fine, axis=-1), FINE_TOP_K)
    top_p = top_p / jnp.sum(top_p, axis=-1, keepdims=True)
    expert_id = grp[:, None] * EXPERTS_PER_GROUP + top_i
    weights = w_grp * top_p
    combine = jnp.sum(jax.nn.one_hot(expert_id, N_EXPERTS, dtype=jnp.float32) * weights[..., None], axis=1)
    combine = combine.astype(h.dtype)
    y = jnp.zeros_like(ht)
    for e in range(N_EXPERTS):
        he = jax.nn.silu(ht @ w_gate[e]) * (ht @ w_up[e])
        y = y + combine[:, e:e + 1] * (he @ w_down[e])
    return y.reshape(bsz, T, D)

def setup_inputs(seed: int = 0) -> dict:
    key = jax.random.key(seed)
    ks = list(jax.random.split(key, 32))
    def nrm(shape, scale):
        return jax.random.normal(ks.pop(), shape, jnp.float32) * scale
    def gain(shape):
        return 1.0 + nrm(shape, 0.02)
    L, D = DEPTH, D_MODEL
    x = nrm((BATCH, SEQ, D), 1.0)
    mem = nrm((BATCH, MEM_LEN, D), 1.0)
    mix_norm_g = gain((L, D))
    w_in = nrm((L, D, IN_WIDTH), D ** -0.5)
    fox_forget_b = jax.random.uniform(ks.pop(), (L, FOX_HEADS), jnp.float32, 1.0, 4.0)
    pool_w = nrm((L, POOL_GROUPS, POOL_GROUP_DIM, POOL_GROUP_DIM), POOL_GROUP_DIM ** -0.5)
    pool_scale = 1.0 + nrm((L, POOL_WIDTH), 0.1)
    cmp_pe_k = nrm((L, CMP_LEN, HEAD_DIM), 0.02)
    cmp_pe_v = nrm((L, CMP_LEN, HEAD_DIM), 0.02)
    cmp_w1_k = nrm((L, CMP_LEN * HEAD_DIM, CMP_HIDDEN), (CMP_LEN * HEAD_DIM) ** -0.5)
    cmp_w2_k = nrm((L, CMP_HIDDEN, HEAD_DIM), CMP_HIDDEN ** -0.5)
    cmp_w1_v = nrm((L, CMP_LEN * HEAD_DIM, CMP_HIDDEN), (CMP_LEN * HEAD_DIM) ** -0.5)
    cmp_w2_v = nrm((L, CMP_HIDDEN, HEAD_DIM), CMP_HIDDEN ** -0.5)
    nsa_gate_b = nrm((L, NSA_HEADS * N_BRANCH), 0.01)
    w_out = nrm((L, MIX_WIDTH, D), MIX_WIDTH ** -0.5)
    xattn_norm_g = gain((L, D))
    mem_norm_g = gain((L, D))
    xattn_wq = nrm((L, D, D), D ** -0.5)
    xattn_wk = nrm((L, D, D), D ** -0.5)
    xattn_wv = nrm((L, D, D), D ** -0.5)
    xattn_wo = nrm((L, D, D), D ** -0.5)
    ffn_norm_g = gain((L, D))
    router_coarse_w = nrm((L, D, N_GROUPS), D ** -0.5)
    router_coarse_b = nrm((L, N_GROUPS), 0.01)
    router_fine_w = nrm((L, D, N_EXPERTS), D ** -0.5)
    router_fine_b = nrm((L, N_EXPERTS), 0.01)
    exp_w_gate = nrm((L, N_EXPERTS, D, EXPERT_FF), D ** -0.5)
    exp_w_up = nrm((L, N_EXPERTS, D, EXPERT_FF), D ** -0.5)
    exp_w_down = nrm((L, N_EXPERTS, EXPERT_FF, D), EXPERT_FF ** -0.5)
    final_norm_g = gain((D,))
    return {"x": x, "mem": mem, "mix_norm_g": mix_norm_g, "w_in": w_in, "fox_forget_b": fox_forget_b,
            "pool_w": pool_w, "pool_scale": pool_scale, "cmp_pe_k": cmp_pe_k, "cmp_pe_v": cmp_pe_v,
            "cmp_w1_k": cmp_w1_k, "cmp_w2_k": cmp_w2_k, "cmp_w1_v": cmp_w1_v, "cmp_w2_v": cmp_w2_v,
            "nsa_gate_b": nsa_gate_b, "w_out": w_out, "xattn_norm_g": xattn_norm_g, "mem_norm_g": mem_norm_g,
            "xattn_wq": xattn_wq, "xattn_wk": xattn_wk, "xattn_wv": xattn_wv, "xattn_wo": xattn_wo,
            "ffn_norm_g": ffn_norm_g, "router_coarse_w": router_coarse_w, "router_coarse_b": router_coarse_b,
            "router_fine_w": router_fine_w, "router_fine_b": router_fine_b, "exp_w_gate": exp_w_gate,
            "exp_w_up": exp_w_up, "exp_w_down": exp_w_down, "final_norm_g": final_norm_g}

def reference(x, mem, mix_norm_g, w_in, fox_forget_b, pool_w, pool_scale, cmp_pe_k, cmp_pe_v,
              cmp_w1_k, cmp_w2_k, cmp_w1_v, cmp_w2_v, nsa_gate_b, w_out, xattn_norm_g, mem_norm_g,
              xattn_wq, xattn_wk, xattn_wv, xattn_wo, ffn_norm_g, router_coarse_w, router_coarse_b,
              router_fine_w, router_fine_b, exp_w_gate, exp_w_up, exp_w_down, final_norm_g):
    pts = _split_points()
    for l in range(DEPTH):
        h = rms_norm(x, mix_norm_g[l])
        (qa, ka, va, fa, ub, qc, kcm, vcm, ksl, vsl, kwn, vwn, gl) = jnp.split(h @ w_in[l], pts, axis=-1)
        o_a = fox_attention(qa, ka, va, fa, fox_forget_b[l])
        o_b = pool_mixer(ub, pool_w[l], pool_scale[l])
        o_c = nsa_attention(qc, kcm, vcm, ksl, vsl, kwn, vwn, gl, nsa_gate_b[l],
                            cmp_pe_k[l], cmp_pe_v[l], cmp_w1_k[l], cmp_w2_k[l], cmp_w1_v[l], cmp_w2_v[l])
        x = x + jnp.concatenate([o_a, o_b.astype(o_a.dtype), o_c], axis=-1) @ w_out[l]
        x = x + memory_cross_attention(rms_norm(x, xattn_norm_g[l]), rms_norm(mem, mem_norm_g[l]),
                                       xattn_wq[l], xattn_wk[l], xattn_wv[l], xattn_wo[l])
        x = x + hier_moe(rms_norm(x, ffn_norm_g[l]), router_coarse_w[l], router_coarse_b[l],
                         router_fine_w[l], router_fine_b[l], exp_w_gate[l], exp_w_up[l], exp_w_down[l])
    return rms_norm(x, final_norm_g)


_drawn_inputs = setup_inputs


def setup_inputs(seed=0):
    import zlib

    import numpy as np

    out = dict(_drawn_inputs(seed))
    spreads = {}
    factors = {'mix_norm_g': 3.265,
     'cmp_pe_k': 8.0,
     'cmp_pe_v': 6.803,
     'nsa_gate_b': 8.0,
     'xattn_norm_g': 8.0,
     'mem_norm_g': 8.0,
     'ffn_norm_g': 2.975,
     'router_coarse_b': 5.874,
     'router_fine_b': 20.254,
     'final_norm_g': 7.733}
    for name, (base, spread) in spreads.items():
        noise = np.random.default_rng([zlib.crc32(name.encode()), seed]).standard_normal(out[name].shape)
        drawn = base * np.exp(spread * noise) if base else spread * noise
        out[name] = __import__('jax').numpy.asarray(drawn.astype(out[name].dtype))
    for name, factor in factors.items():
        out[name] = (out[name] * factor).astype(out[name].dtype)
    return out
```

```python
import concourse.bass as bass
from concourse import mybir
from contextlib import ExitStack

F32 = mybir.dt.float32
F32R = mybir.dt.float32r
BF16 = mybir.dt.bfloat16
I32 = mybir.dt.int32
ALU = mybir.AluOpType
ACT = mybir.ActivationFunctionType
AX = mybir.AxisListType

P = 128
D = 1024
KD = D // P
T = 512
NT = T // P
DH = 64
FOX_H = 6
NSA_H = 6
NSA_G = 2
NSA_R = NSA_H // NSA_G
FOX_W = FOX_H * DH
POOL_W = 256
POOL_WINDOWS = (2, 4, 8, 16)
NSA_W = NSA_H * DH
KV_W = NSA_G * DH
SMALL_W = FOX_H + 3 * NSA_H
CMP_LEN, CMP_STRIDE = 32, 16
N_CMP = T // CMP_STRIDE - 1
CMP_PAD = 32
CMP_HID = 256
MEM = 256
MT = MEM // P
MEM_H = 4
NEXP = 16
NGRP = 4
PER = 4
FF = 512
KF = FF // P
EPS = 1e-6
ROUT_W = NGRP + NEXP

PIECE = 2048
RAW = 3
SPLIT = 2
MRAW, MSPLIT = 6, 3
DRING = 4
CHUNK = P
N_CONST, N_CONST2 = 5, 12
MAXCH = 24


def offsets():
    names = ["fq", "fk", "fv", "ff", "pool", "nq", "kcm", "vcm", "ksl", "vsl", "kwn", "vwn", "gate"]
    widths = [FOX_W, FOX_W, FOX_W, FOX_H, POOL_W, NSA_W] + [KV_W] * 6 + [3 * NSA_H]
    at, out = 0, {}
    for n, w in zip(names, widths):
        out[n] = at
        at += w
    return out


def build(nc, A, C, out):
    O = offsets()
    with ExitStack() as ctx:
        def sb(name, shape, dt=F32):
            return ctx.enter_context(nc.sbuf_tensor(name, shape, dt))

        def sem(name):
            return ctx.enter_context(nc.semaphore(name))

        def dram(name, shape, dt=F32):
            return nc.dram_tensor(name, shape, dt, kind="Internal").ap()

        raw = sb("raw", [P, RAW, PIECE])
        whi = sb("whi", [P, SPLIT, PIECE], F32R)
        wlo = sb("wlo", [P, SPLIT, PIECE], F32R)
        ahi = sb("ahi", [P, KD, T], F32R)
        alo = sb("alo", [P, KD, T], F32R)
        mhi = sb("mhi", [P, KD * MEM], F32R)
        mlo = sb("mlo", [P, KD * MEM], F32R)
        arena = sb("arena", [P, 15040])
        gbc = sb("gbc", [P, D])
        tok = sb("tok", [P, 4, D])
        work = sb("work", [P, 2624])
        ident = sb("ident", [P, P])
        bfc = sb("bfc", [P, 5 * P], BF16)
        wsm = sb("wsm", [P, KD, SMALL_W])
        wsm_hi = sb("wsm_hi", [P, KD, SMALL_W], F32R)
        wsm_lo = sb("wsm_lo", [P, KD, SMALL_W], F32R)
        wrt = sb("wrt", [P, KD, ROUT_W])
        wrt_hi = sb("wrt_hi", [P, KD, ROUT_W], F32R)
        wrt_lo = sb("wrt_lo", [P, KD, ROUT_W], F32R)
        w2 = sb("w2", [P, 2, 2, DH])
        pe2 = sb("pe2", [P, 2, 16])
        wpool = sb("wpool", [P, 2, P])
        gT = sb("gT", [P, 2, 2, 2 * N_CMP])
        pcon = sb("pcon", [P, 2, 17])
        pscale_t = sb("pscale_t", [P, 2])
        bias24 = sb("bias24", [P, SMALL_W])
        rbias = sb("rbias", [P, ROUT_W])
        half = sb("half", [P, 1])
        stat = sb("stat", [P, 3, 20])
        zz = sb("zz", [P, 6, NT, SMALL_W])
        nmax = sb("nmax", [P, 96])
        den = sb("den", [P, 96])
        rden = sb("rden", [P, 96])
        coef = sb("coef", [P, 96])
        cst = sb("cst", [P, 5, 24])
        spare = sb("spare", [P, 2])
        zeroi = sb("zeroi", [P, 1], I32)
        lall = sb("lall", [P, MAXCH + 1, 2], I32)
        xidx = sb("xidx", [P, 1], I32)
        yidx = sb("yidx", [P, 1], I32)
        yw = sb("yw", [P, 1])
        lst = sb("lst", [P, 2 * NT, 2], I32)
        posi = sb("posi", [P, 2 * NT], I32)
        etab = sb("etab", [P, MAXCH + 1], I32)
        tabs = sb("tabs", [P, MAXCH + 4 + NEXP + NT])
        ps = [ctx.enter_context(nc.psum_tensor(f"ps{i}", [P, 512], F32)) for i in range(8)]

        h3d = dram("h3d", [T + P, D])
        xod = dram("xod", [T + P, D])
        lstd = dram("lstd", [(MAXCH + 1) * P, 2], I32)

        def carve(at, *shape):
            n = 1
            for s in shape:
                n *= s
            ap = arena[:, at:at + n]
            if len(shape) == 1:
                return ap, at + n
            names = "abc"[:len(shape)]
            spec = f"p ({' '.join(names)}) -> p {' '.join(names)}"
            return ap.rearrange(spec, **{k: s for k, s in zip(names, shape)}), at + n

        Qf, at = carve(0, FOX_H, T)
        Kf, at = carve(at, FOX_H, T)
        Qn, at = carve(at, NSA_H, T)
        Ks, at = carve(at, NSA_G, T)
        Kw, at = carve(at, NSA_G, T)
        Vf, at = carve(at, NT, FOX_W)
        vs_at = at
        Vs, at = carve(at, NT, KV_W)
        Vw, at = carve(at, NT, KV_W)
        Fb, _ = carve(vs_at, 16, NSA_G, N_CMP)
        Kc, at = carve(at, NSA_G, CMP_PAD)
        Vc, at = carve(at, NSA_G, NSA_R * DH)
        Pc, at = carve(at, NT, NSA_H, CMP_PAD)
        assert at <= 15040
        X, at = carve(0, NT, D)
        QTx, at = carve(at, KD, T)
        KTm, at = carve(at, KD, MEM)
        Vm, at = carve(at, MT, D)
        assert at <= 15040

        raw_x, at = carve(NT * D, MRAW - RAW, PIECE)
        assert at <= NT * D + KD * (T + MEM)

        KG = [tok[:, b, :].rearrange("p (g t) -> p g t", g=NSA_G) for b in range(2)]
        Pr = [work[:, 512 * b:512 * b + 512] for b in range(3)]
        PTr = [work[:, 1536 + 512 * b:2048 + 512 * b] for b in range(2)]
        tri = work[:, 0:T]
        UW = T + 16
        bf_stage = work[:, 640:640 + 5 * P]
        cumr = work[0:FOX_H, 1600:1600 + 2 * T].rearrange("p (b t) -> p b t", b=2)
        Ub, Sa, Sb = (work[:, UW * b:UW * (b + 1)] for b in range(3))
        pooled = work[:, 3 * UW:3 * UW + 2 * T].rearrange("p (f t) -> p f t", f=2)
        identb, maskb, maskc, sut, ones = (bfc[:, P * b:P * (b + 1)] for b in range(5))
        invw, corr, pscale = pcon[:, :, 0:1], pcon[:, :, 1:17], pscale_t[:, :].unsqueeze(2)
        fhi = [mhi[:, 992 * b:992 * (b + 1)].rearrange("p (j m) -> p j m", j=16) for b in range(2)]
        flo = [mlo[:, 992 * b:992 * (b + 1)].rearrange("p (j m) -> p j m", j=16) for b in range(2)]
        memhi = mhi[:, :].rearrange("p (k t) -> p k t", k=KD)
        memlo = mlo[:, :].rearrange("p (k t) -> p k t", k=KD)
        xghi = mhi[:, 0:KD * P].rearrange("p (k t) -> p k t", k=KD)
        xglo = mlo[:, 0:KD * P].rearrange("p (k t) -> p k t", k=KD)
        hehi = mhi[:, KD * P:KD * P + KF * P].rearrange("p (k t) -> p k t", k=KF)
        helo = mlo[:, KD * P:KD * P + KF * P].rearrange("p (k t) -> p k t", k=KF)
        sg, he = work[:, 0:FF], work[:, FF:2 * FF]
        hgrid, tiew, eiota, tokid = (tabs[:, 0:MAXCH], tabs[:, MAXCH:MAXCH + 4],
                                     tabs[:, MAXCH + 4:MAXCH + 4 + NEXP], tabs[:, MAXCH + 4 + NEXP:])

        def cols(w, c0, n):
            return w[:, c0:c0 + n].rearrange("(k p) n -> p k n", p=P)

        win, wout = A["w_in"][0], A["w_out"][0]
        wq, wk, wv, wo = (A[f"xattn_w{c}"][0] for c in "qkvo")
        pieces = []
        groups = []
        KEY = {}

        def piece(key, loads, grps):
            KEY[key] = len(pieces)
            for kind, idx, c0, n, eng in grps:
                groups.append((len(pieces), kind, idx, c0, n, eng))
            pieces.append(loads)

        def two(key, w, c0, eng="act"):
            piece(key, [(0, cols(w, c0, 256))], [("F", f, f * P, P, eng) for f in range(2)])

        def pair(key, w, c0, c1):
            piece(key, [(0, cols(w, c0, P)), (P, cols(w, c1, P))], [("F", f, f * P, P, "act") for f in range(2)])

        two("fq0", win, O["fq"])
        pair("fq1", win, O["fq"] + 256, O["kcm"])
        two("fk0", win, O["fk"])
        pair("fk1", win, O["fk"] + 256, O["vcm"])
        two("pool", win, O["pool"], "dve")
        two("nq0", win, O["nq"])
        for kv, w in enumerate((A["cmp_w1_k"][0], A["cmp_w1_v"][0])):
            wv_ = w.rearrange("(j p) n -> p j n", p=P)
            for b in range(2):
                piece(f"c{kv}{b}", [(0, wv_[:, 8 * b:8 * b + 8, :])], [("C", 2 * kv + b, 0, 0, None)])
        pair("nq1", win, O["nq"] + 256, O["ksl"])
        piece("fv0", [(0, cols(win, O["fv"], 256))], [("T", t, 0, 256, "act") for t in range(NT)])
        piece("fv1", [(0, cols(win, O["fv"] + 256, P)), (P, cols(win, O["vsl"], P))],
              [("T", t, 0, 256, "act") for t in range(NT)])
        piece("win", [(0, cols(win, O["kwn"], P)), (P, cols(win, O["vwn"], P))],
              [("F", 0, 0, P, "act")] + [("T", t, P, P, "act") for t in range(NT)])
        for b in range(4):
            piece(f"out{b}", [(0, cols(wout, 256 * b, 256))], [("T", t, 0, 256, "dve") for t in range(NT)])
        for b in range(4):
            piece(f"mk{b}", [(0, cols(wk, 256 * b, 256))], [("F", f, f * P, P, "act") for f in range(2)])
        for b in range(4):
            piece(f"mv{b}", [(0, cols(wv, 256 * b, 256))], [("T", t, 0, 256, "act") for t in range(MT)])
        for b in range(4):
            two(f"xq{b}", wq, 256 * b)
        for b in range(4):
            piece(f"xo{b}", [(0, cols(wo, 256 * b, 256))], [("T", t, 0, 256, "dve") for t in range(NT)])
        ND = len(pieces)
        NMP = ND + 4
        ORDER = sorted(KEY, key=KEY.get)
        of_piece = [[g for g, x in enumerate(groups) if x[0] == n] for n in range(ND)]
        raw_need = []
        for n in range(ND):
            before = raw_need[n - RAW] if n >= RAW else 0
            raw_need.append(before + 16 * len(pieces[n]))

        def moe_raw(m):
            i = m % MRAW
            return raw[:, (ND + i) % RAW, :] if i < RAW else raw_x[:, i - RAW, :]

        def moe_full(m):
            i = m % MRAW
            if i < RAW:
                return raw_full[(ND + i) % RAW], raw_need[ND - RAW + i] + 16 * (m // MRAW + 1)
            return rawx_full[i - RAW], 16 * (m // MRAW + 1)

        def moe_split(m):
            i = m % MSPLIT
            if i < SPLIT:
                return whi[:, (ND + i) % SPLIT, :], wlo[:, (ND + i) % SPLIT, :]
            flat = "p k t -> p (k t)"
            return ahi[:, 0:PIECE // T, :].rearrange(flat), alo[:, 0:PIECE // T, :].rearrange(flat)

        def evacs(g, eng):
            return sum(x[5] == eng for x in groups[:g + 1])

        UN = []
        for i in range(NT):
            UN += [(i, "c", g, 0) for g in range(NSA_G)] + [(i, "f", h, i + 1) for h in range(FOX_H)]
            UN += [(i, b, h, i + 1) for h in range(NSA_H) for b in "sw"]
        UX = [(i, "x", h, MT) for i in range(NT) for h in range(MEM_H)]

        class Phase:

            def __init__(self, name, units, col0):
                self.units = units
                self.per = len(units) // NT
                self.col0 = col0
                self.sidx = []
                n = 0
                for x in units:
                    self.sidx.append(n)
                    n += x[1] != "c"
                self.of_s = [u for u, x in enumerate(units) if x[1] != "c"]
                self.scores_done = sem(name + "_scores_done")
                self.max_done = sem(name + "_max_done")
                self.exp_done = sem(name + "_exp_done")
                self.tp_done = sem(name + "_tp_done")
                self.pt_done = sem(name + "_pt_done")
                self.pv_done = sem(name + "_pv_done")
                self.o_done = sem(name + "_o_done")
                self.ot_done = sem(name + "_ot_done")
                self.ot_hi = sem(name + "_ot_hi")
                self.ot_lo = sem(name + "_ot_lo")
                self.blocks = ([list(range(3)), list(range(5, 8))] if name == "A"
                               else [list(range(4)), list(range(4, 8))])
                self.steps = len(units) + 8

            def score(self, u):
                return 0 <= u < len(self.units) and self.units[u][1] != "c"

            def has(self, u):
                return 0 <= u < len(self.units)

            def rounds(self, k):
                return [(2 * i + b, i, self.blocks[b]) for i in range(NT) for b in range(2)
                        if k == self.per * (i + 1) + 4 + 2 * b]

        PA = Phase("A", UN, 0)
        PX = Phase("X", UX, 72)

        raw_full = [sem(f"raw_full{i}") for i in range(RAW)]
        rawx_full = [sem(f"rawx_full{i}") for i in range(MRAW - RAW)]
        hi_done = sem("hi_done")
        lo_done = sem("lo_done")
        grp_done = sem("grp_done")
        evac = {"act": sem("evac_act"), "dve": sem("evac_dve")}
        ident_in = sem("ident_in")
        const_in = sem("const_in")
        const2_in = sem("const2_in")
        small_in = sem("small_in")
        rows_in = sem("rows_in")
        xin_full = [sem(f"xin_full{i}") for i in range(2)]
        gain_full = sem("gain_full")
        ss_done = sem("ss_done")
        ms_done = sem("ms_done")
        rms_done = sem("rms_done")
        h_done = sem("h_done")
        ntp_done = sem("ntp_done")
        ntp_hi = sem("ntp_hi")
        ntp_lo = sem("ntp_lo")
        half_set = sem("half_set")
        bf_done = sem("bf_done")
        sm_hi = sem("sm_hi")
        sm_lo = sem("sm_lo")
        small_mm = sem("small_mm")
        z_done = sem("z_done")
        zexp_done = sem("zexp_done")
        lf_done = sem("lf_done")
        gate_done = sem("gate_done")
        cum_mm = sem("cum_mm")
        cum_done = sem("cum_done")
        cumrow_in = sem("cumrow_in")
        kg_done = sem("kg_done")
        f_done = sem("f_done")
        fhi_done = sem("fhi_done")
        flo_done = sem("flo_done")
        steps = sem("pool_steps")
        gelu_done = sem("gelu_done")
        kv2_mm = sem("kv2_mm")
        kc_done = sem("kc_done")
        vc_done = sem("vc_done")
        pad_done = sem("pad_done")
        cs_done = sem("cs_done")
        csub_done = sem("csub_done")
        cexp_done = sem("cexp_done")
        pc_done = sem("pc_done")
        pooled_done = sem("pooled_done")
        mix_mm = sem("mix_mm")
        mix_hi = sem("mix_hi")
        mix_lo = sem("mix_lo")
        x_in = [sem(f"x_in{t}") for t in range(NT)]
        dch = sem("dve_chain")
        ach = sem("act_chain")
        route_mm = sem("route_mm")
        r_step = sem("r_step")
        r_exp = sem("r_exp")
        onehot_done = sem("onehot_done")
        rank_mm = sem("rank_mm")
        route_done = sem("route_done")
        list_init = sem("list_init")
        zero_done = sem("zero_done")
        zero_out = sem("zero_out")
        h3_out = [sem(f"h3_out{t}") for t in range(NT)]
        xo_out = sem("xo_out")
        scat_done = sem("scat_done")
        list_in = sem("list_in")
        yw_done = sem("yw_done")
        xg_in = sem("xg_in")
        used = sem("moe_piece_used")
        xg_tp = sem("xg_tp")
        xg_hi = sem("xg_hi")
        xg_lo = sem("xg_lo")
        silu_done = sem("silu_done")
        he_done = sem("he_done")
        he_tp = sem("he_tp")
        he_hi = sem("he_hi")
        he_lo = sem("he_lo")
        y_done = sem("y_done")
        y_out = sem("y_out")
        adds_done = sem("adds_done")
        out_done = [sem(f"out_done{t}") for t in range(NT)]

        NX, NM, N2, N3, N4 = 0, NT, NT + MT, 2 * NT + MT, 3 * NT + MT

        block = ctx.enter_context(nc.Block())

        def wait_consumed(eng, n):
            eng.wait_ge(grp_done, of_piece[n][-1] + 1)

        @block.sync
        def _(sp):
            def load_piece(n):
                if n >= RAW:
                    sp.wait_ge(lo_done, n - RAW + 1)
                for c0, src in pieces[n]:
                    w = src.shape[2]
                    dst = raw[:, n % RAW, :].rearrange("p (k n) -> p k n", k=KD)[:, :, c0:c0 + w]
                    sp.dma_start(dst, src).then_inc(raw_full[n % RAW], 16)

            def load_tok(q, src):
                if q >= 2:
                    sp.wait_ge(h_done, q - 1)
                sp.dma_start(tok[:, q % 2, :], src).then_inc(xin_full[q % 2], 16)

            x_t = A["x"][0].rearrange("(t p) d -> t p d", p=P)
            m_t = A["mem"][0].rearrange("(t p) d -> t p d", p=P)
            for t in range(2):
                load_tok(NX + t, x_t[t])
            load_piece(0)
            for t in range(2, NT):
                load_tok(NX + t, x_t[t])
            sp.dma_start(wsm[:, :, 0:FOX_H], cols(win, O["ff"], FOX_H)).then_inc(small_in, 16)
            sp.dma_start(wsm[:, :, FOX_H:SMALL_W], cols(win, O["gate"], 3 * NSA_H)).then_inc(small_in, 16)
            sp.dma_start(wrt[:, :, 0:NGRP], cols(A["router_coarse_w"][0], 0, NGRP)).then_inc(small_in, 16)
            sp.dma_start(wrt[:, :, NGRP:ROUT_W], cols(A["router_fine_w"][0], 0, NEXP)).then_inc(small_in, 16)
            for n in range(1, KEY["out0"]):
                load_piece(n)
                if n == 3:
                    sp.wait_ge(cum_done, 2)
                    sp.dma_start(Qf[64:65, :, :], cumr[:, 0, :]).then_inc(cumrow_in, 16)
                    sp.dma_start(Kf[65:66, :, :], cumr[:, 1, :]).then_inc(cumrow_in, 16)
            sp.wait_ge(f_done, 2)
            for t in range(MT):
                load_tok(NM + t, m_t[t])
            for n in range(KEY["out0"], KEY["out1"] + 1):
                load_piece(n)
            last_fox = max(u for u, x in enumerate(UN) if x[1] == "f")
            sp.wait_ge(PA.scores_done, PA.sidx[last_fox] + 1)
            for t in range(NT):
                sp.dma_start(X[:, t, :], x_t[t]).then_inc(x_in[t], 16)
            for n in range(KEY["out1"] + 1, ND):
                load_piece(n)
            wg, wu, wd = (A[f"exp_w_{c}"][0] for c in ("gate", "up", "down"))

            def load_expert(w, e, half_, m):
                src = w[bass.ds(e, 1), :, :].rearrange("e (k p) f -> p (e k) f", p=P)
                if w is wd:
                    src = src[:, :, 512 * half_:512 * half_ + 512]
                else:
                    src = src[:, KF * half_:KF * half_ + KF, :]
                dst = moe_raw(m).rearrange("p (k f) -> p k f", k=KF)
                sp.dma_start(dst, src).then_inc(moe_full(m)[0], 16)

            for m, w in enumerate((wg, wg, wu, wu)):
                if m < RAW:
                    sp.wait_ge(lo_done, ND + m - RAW + 1)
                else:
                    sp.wait_ge(grp_done, of_piece[KEY["xo0"]][0] + 1)
                load_expert(w, 0, m % 2, m)
            sp.wait_ge(route_done, 1)
            turns = sp.value_load(etab[0:1, MAXCH:MAXCH + 1], min_val=NEXP - 2, max_val=MAXCH - 3)
            with sp.Fori(1, turns + 2) as j:
                e = sp.value_load(etab[0:1, bass.ds(j, 1)], min_val=0, max_val=NEXP - 1)
                ep = sp.value_load(etab[0:1, bass.ds(j - 1, 1)], min_val=0, max_val=NEXP - 1)
                for i, (w, x) in enumerate(((wg, e), (wg, e), (wu, e), (wu, e), (wd, ep), (wd, ep))):
                    sp.wait_ge(lo_done, 6 * (j - 1) + (NMP + i - MRAW + 1))
                    load_expert(w, x, i % 2, 4 + i)
            ep = sp.value_load(etab[0:1, bass.ds(turns + 1, 1)], min_val=0, max_val=NEXP - 1)
            for i in range(2):
                sp.wait_ge(lo_done, 6 * turns + (NMP + 6 + i - MRAW + 1))
                load_expert(wd, ep, i, 10 + i)
            sp.wait_ge(adds_done, 1)
            xo_t = xod[0:T, :].rearrange("(t p) d -> t p d", p=P)
            out_t = out[0].rearrange("(t p) d -> t p d", p=P)
            for t in range(2):
                load_tok(N4 + t, xo_t[t])
            for t in range(NT):
                sp.wait_ge(h_done, N4 + t + 1)
                sp.dma_start(out_t[t], tok[:, 2 + (N4 + t) % 2, :]).then_inc(out_done[t], 16)
                if t + 2 < NT:
                    load_tok(N4 + t + 2, xo_t[t + 2])
            for t in range(NT):
                sp.wait_ge(out_done[t], 16)

        @block.gpsimd
        def _(pool):
            pool.memset(half[:, :], -0.5).then_inc(half_set, 1)
            pool.memset(spare[:, 0:1], 0.0).then_inc(half_set, 1)
            pool.memset(zeroi[:, :], 0).then_inc(half_set, 1)
            pool.wait_ge(half_set, 3)

            def rms(q):
                pool.wait_ge(ms_done, q + 1)
                pool.tensor_tensor(stat[:, 2, q:q + 1], stat[:, 1, q:q + 1], half[:, :], ALU.pow).then_inc(rms_done, 1)

            for q in range(NT):
                rms(q)
            pool.dma_start(tri, C["tri"]).then_inc(const_in, 16)
            pool.dma_start(bias24[:, 0:FOX_H], A["fox_forget_b"].to_broadcast([P, FOX_H])).then_inc(const_in, 16)
            pool.dma_start(bias24[:, FOX_H:], A["nsa_gate_b"].to_broadcast([P, 3 * NSA_H])).then_inc(const_in, 16)
            for kv, c in enumerate("kv"):
                pool.dma_start(pe2[:, kv, :], A[f"pe_{c}"]).then_inc(const_in, 16)
            pool.dma_start(bf_stage, C["bf"]).then_inc(const2_in, 16)
            pool.dma_start(pcon[:, :, :], C["pool"]).then_inc(const2_in, 16)
            pool.dma_start(pscale_t[:, :], A["pscale"]).then_inc(const2_in, 16)
            for kv, c in enumerate("kv"):
                pool.dma_start(w2[:, kv, :, :], A[f"cmp_w2_{c}"][0].rearrange("(k p) n -> p k n", p=P))\
                    .then_inc(const2_in, 16)
            pool.wait_ge(pad_done, 1)
            for g in range(4):
                lo = DH * (g % 2)
                pool.dma_start(wpool[lo:lo + DH, g // 2, lo:lo + DH], A["pool_w"][0, g]).then_inc(const2_in, 16)
            pool.dma_start(tabs[:, :], C["tabs"]).then_inc(const2_in, 16)
            pool.dma_start(rbias[:, 0:NGRP], A["router_coarse_b"].to_broadcast([P, NGRP])).then_inc(const2_in, 16)
            pool.dma_start(rbias[:, NGRP:], A["router_fine_b"].to_broadcast([P, NEXP])).then_inc(const2_in, 16)
            pool.dma_start(Qn[64:66, :, :], C["qrows"]).then_inc(rows_in, 16)
            pool.dma_start(Ks[64:66, :, :], C["krows"]).then_inc(rows_in, 16)
            pool.dma_start(Kw[64:66, :, :], C["krows"]).then_inc(rows_in, 16)
            pool.dma_start(Kc[64:66, :, :], C["crows"]).then_inc(rows_in, 16)
            pool.dma_start(Qf[65:66, :, :], C["ones"]).then_inc(rows_in, 16)
            pool.dma_start(Kf[64:65, :, :], C["ones"]).then_inc(rows_in, 16)
            pool.dma_start(lstd, C["list"]).then_inc(list_init, 16)
            for q in range(NT, N4):
                rms(q)
            pool.wait_ge(route_done, 1)
            pool.wait_ge(list_init, 16)
            for m in range(2 * NT):
                pool.indirect_dma_start(lstd, bass.IndirectOffsetOnAxis(ap=posi[:, m:m + 1], axis=0),
                                        lst[:, m, :], None).then_inc(scat_done, 16)
            turns = pool.value_load(etab[0:1, MAXCH:MAXCH + 1], min_val=NEXP - 2, max_val=MAXCH - 3)
            pool.wait_ge(scat_done, 16 * 2 * NT)
            pool.wait_ge(zero_out, 32)
            for t in range(NT):
                pool.wait_ge(h3_out[t], 16)
            pool.wait_ge(xo_out, 16 * NT)

            pool.dma_start(lall[:, :, :], lstd.rearrange("(c p) w -> p c w", p=P)).then_inc(list_in, 16)
            pool.wait_ge(list_in, 16)

            def copy_tokens(dst, c):
                pool.tensor_tensor(dst[:, :], lall[:, bass.ds(c, 1), 0], zeroi[:, :], ALU.add).then_inc(steps, 1)

            def copy_weights(c):
                pool.tensor_tensor(yw[:, :], lall[:, bass.ds(c, 1), 1].bitcast(F32), spare[:, 0:1], ALU.add)\
                    .then_inc(yw_done, 1)

            def pause():
                pool.tensor_tensor(spare[:, 1:2], spare[:, 0:1], spare[:, 0:1], ALU.add).then_inc(steps, 1)

            def gather():
                pool.indirect_dma_start(tok[:, 0, :], None, h3d,
                                        bass.IndirectOffsetOnAxis(ap=xidx[:, :], axis=0)).then_inc(xg_in, 16)

            def add():
                pool.indirect_dma_start(xod, bass.IndirectOffsetOnAxis(ap=yidx[:, :], axis=0),
                                        tok[:, 2, :], None, compute_op=ALU.add).then_inc(y_out, 16)

            for c in range(3):
                if c:
                    pool.wait_ge(xg_in, 16 * c)
                    pool.wait_ge(xg_tp, 2 * c)
                copy_tokens(xidx, c)
                pool.wait_ge(steps, c + 1)
                gather()
            copy_weights(0)
            with pool.Fori(1, turns + 2) as j:
                pool.wait_ge(xg_in, 16 * j + 32)
                pool.wait_ge(xg_tp, 2 * j + 4)
                copy_tokens(xidx, j + 2)
                pool.wait_ge(steps, 4 * j)
                pause()
                gather()
                copy_tokens(yidx, j - 1)
                pool.wait_ge(steps, 4 * j + 2)
                pool.wait_ge(y_done, 2 * j)
                pause()
                add()
                pool.wait_ge(y_out, 16 * j)
                copy_weights(j)
            copy_tokens(yidx, turns + 1)
            pool.wait_ge(steps, 4 * turns + 8)
            pool.wait_ge(y_done, 2 * turns + 4)
            pause()
            add()
            pool.wait_ge(y_out, 16 * turns + 32)
            pool.wait_ge(xg_in, 16 * turns + 64)
            pool.wait_ge(steps, 4 * turns + 9)
            pool.tensor_tensor(spare[:, 1:2], spare[:, 0:1], spare[:, 0:1], ALU.add).then_inc(adds_done, 1)
            for q in range(N4, N4 + NT):
                rms(q)

        @block.scalar
        def _(act):
            a = nc.scalar
            chain = [0]

            def link(ins):
                chain[0] += 1
                ins.then_inc(ach, 1)
                act.wait_ge(ach, chain[0])

            act.dma_start(ident[:, :], C["ident"]).then_inc(ident_in, 16)
            g_mix, g_x, g_m, g_f, g_o = (A[n] for n in ("mix_norm_g", "xattn_norm_g", "mem_norm_g", "ffn_norm_g",
                                                        "final_norm_g"))
            act.dma_start(gbc[:, :], g_mix.to_broadcast([P, D])).then_inc(gain_full, 16)

            def split(n):
                act.wait_ge(raw_full[n % RAW], raw_need[n])
                if n >= SPLIT:
                    wait_consumed(act, n - SPLIT)
                a.activation(whi[:, n % SPLIT, :], raw[:, n % RAW, :], ACT.Copy).then_inc(hi_done, 1)

            def split_expert(m, j=None):
                full, need = moe_full(m)
                act.wait_ge(full, need if j is None else 16 * (j - 1) + need)
                if m < SPLIT:
                    wait_consumed(act, ND + m - SPLIT)
                elif m < MSPLIT:
                    act.wait_ge(route_mm, 1)
                else:
                    free = m - MSPLIT + 1
                    act.wait_ge(used, free if j is None else 6 * (j - 1) + free)
                a.activation(moe_split(m)[0], moe_raw(m), ACT.Copy).then_inc(hi_done, 1)

            def square(q, src):
                if q >= 2 and q < N4:
                    act.wait_ge(ntp_done, 2 * (q - 1))
                a.activation(tok[:, 2 + q % 2, :], src, ACT.Square, accum_out=stat[:, 0, q:q + 1]).then_inc(ss_done, 1)

            def norm_hi(q, dst, t):
                for b in range(2):
                    act.wait_ge(ntp_done, 2 * q + b + 1)
                    src = ps[4 + 2 * (q % 2) + b][:, :].rearrange("p (k t) -> p k t", k=4)
                    a.activation(dst[:, 4 * b:4 * b + 4, t * P:(t + 1) * P], src, ACT.Copy).then_inc(ntp_hi, 1)

            def heads_out(dst, h0, bank, scale, last_inc=True):
                a.activation(dst[0:64, h0, :], bank[0:64, :], ACT.Copy, scale=scale)
                return a.activation(dst[0:64, h0 + 1, :], bank[64:128, :], ACT.Copy, scale=scale)

            def compress_in(kv, bank):
                for g in range(NSA_G):
                    a.activation(KG[kv][0:64, g, :], bank[64 * g:64 * g + 64, :], ACT.Copy)
                    ins = a.activation(KG[kv][64:128, g, 0:T - 1], bank[64 * g:64 * g + 64, 1:T], ACT.Copy)
                return ins

            def evacuate(n):
                key = ORDER[n]
                for g in of_piece[n]:
                    _, kind, idx, c0, w, eng = groups[g]
                    if eng != "act":
                        continue
                    act.wait_ge(grp_done, g + 1)
                    b = ps[g % DRING]
                    if key == "fq0":
                        ins = heads_out(Qf, 2 * idx, b, DH ** -0.5)
                    elif key == "fk0":
                        ins = heads_out(Kf, 2 * idx, b, 1.0)
                    elif key in ("fq1", "fk1"):
                        kv = key == "fk1"
                        if idx == 0:
                            ins = heads_out(Kf if kv else Qf, 4, b, 1.0 if kv else DH ** -0.5)
                        else:
                            ins = compress_in(int(kv), b)
                    elif key == "nq0":
                        ins = heads_out(Qn, 2 * idx, b, DH ** -0.5)
                    elif key == "nq1":
                        ins = heads_out(Qn, 4, b, DH ** -0.5) if idx == 0 else heads_out(Ks, 0, b, 1.0)
                    elif key == "fv0":
                        ins = a.activation(Vf[:, idx, 0:256], b[:, 0:256], ACT.Copy)
                    elif key == "fv1":
                        a.activation(Vf[:, idx, 256:384], b[:, 0:P], ACT.Copy)
                        ins = a.activation(Vs[:, idx, :], b[:, P:2 * P], ACT.Copy)
                    elif key == "win":
                        ins = heads_out(Kw, 0, b, 1.0) if kind == "F" else \
                            a.activation(Vw[:, idx, :], b[:, 0:P], ACT.Copy)
                    elif key[:2] == "mk":
                        ins = a.activation(KTm[:, 2 * int(key[2]) + idx, :], b[:, 0:MEM], ACT.Copy)
                    elif key[:2] == "mv":
                        c = 256 * int(key[2])
                        ins = a.activation(Vm[:, idx, c:c + 256], b[:, 0:256], ACT.Copy)
                    else:
                        assert key[:2] == "xq"
                        ins = a.activation(QTx[:, 2 * int(key[2]) + idx, :], b[:, :], ACT.Copy,
                                           scale=(D // MEM_H) ** -0.5)
                    ins.then_inc(evac["act"], 1)

            def dense(n):
                evacuate(n)
                if n + SPLIT < ND:
                    split(n + SPLIT)
                else:
                    split_expert(n + SPLIT - ND)

            for t in range(NT):
                act.wait_ge(xin_full[t % 2], 16 * (t // 2 + 1))
                square(NX + t, tok[:, t % 2, :])
                if t == 0:
                    split(0)
                if t >= 1:
                    norm_hi(NX + t - 1, ahi, t - 1)
            norm_hi(NX + NT - 1, ahi, NT - 1)
            split(1)
            act.wait_ge(small_in, 16 * 4)
            a.activation(wsm_hi[:, :, :], wsm[:, :, :], ACT.Copy).then_inc(sm_hi, 1)
            a.activation(wrt_hi[:, :, :], wrt[:, :, :], ACT.Copy).then_inc(sm_hi, 1)
            dense(0)
            act.wait_ge(z_done, 1)
            a.activation(zz[:, 2, :, :], zz[:, 1, :, :], ACT.Exp).then_inc(zexp_done, 1)
            act.wait_ge(zexp_done, 1)
            a.activation(zz[:, 3, :, 0:FOX_H], zz[:, 2, :, 0:FOX_H], ACT.Ln, bias=1.0).then_inc(zexp_done, 1)
            dense(1)
            act.wait_ge(cum_mm, 1)
            a.activation(cumr[:, 0, :], ps[5][0:FOX_H, :], ACT.Copy).then_inc(cum_done, 1)
            a.activation(cumr[:, 1, :], ps[5][0:FOX_H, :], ACT.Copy, scale=-1.0).then_inc(cum_done, 1)
            act.wait_ge(f_done, 1)
            a.activation(fhi[0].rearrange("p j m -> p (j m)"), Fb.rearrange("p a b c -> p (a b c)"),
                         ACT.Copy).then_inc(fhi_done, 1)
            dense(2)
            dense(3)
            act.wait_ge(f_done, 2)
            a.activation(fhi[1].rearrange("p j m -> p (j m)"), Fb.rearrange("p a b c -> p (a b c)"),
                         ACT.Copy).then_inc(fhi_done, 1)
            for n in range(4, KEY["out0"]):
                dense(n)
                key = ORDER[n]
                if key in ("c01", "c11"):
                    kv = int(key[1])
                    for hb in range(2):
                        act.wait_ge(grp_done, of_piece[n][-1] + 1)
                        ins = a.activation(gT[:, kv, hb, :], ps[6 + hb][:, 0:2 * N_CMP], ACT.Gelu_apprx_tanh)
                    ins.then_inc(gelu_done, 1)
            act.wait_ge(kv2_mm, 2)
            act.wait_ge(pad_done, 1)
            a.activation(Kc[0:64, :, 0:N_CMP], ps[4][0:64, 0:2 * N_CMP].rearrange("p (g c) -> p g c", g=NSA_G),
                         ACT.Copy).then_inc(kc_done, 1)
            for b in range(2):
                act.wait_ge(csub_done, b + 1)
                v = Pc[:, :, NSA_R * b:NSA_R * (b + 1), :]
                a.activation(v, v, ACT.Exp).then_inc(cexp_done, 1)
            act.wait_ge(const2_in, 16 * N_CONST2)
            for f in range(2):
                act.wait_ge(mix_mm, f + 1)
                a.activation(ahi[:, 3 + f, :], ps[4 + f][:, :], ACT.Copy, scale=pscale[:, f, :]).then_inc(mix_hi, 1)

            def attention(ph):
                for k in range(ph.steps):
                    if ph.score(k):
                        s = ph.sidx[k]
                        nk = P * ph.units[k][3]
                        act.wait_ge(ph.max_done, s + 1)
                        if s >= 3:
                            act.wait_ge(ph.tp_done, ph.of_s[s - 3] + 1)
                        c = ph.col0 + s
                        a.activation(Pr[s % 3][:, 0:nk], ps[s % 3][:, 0:nk], ACT.Exp, bias=nmax[:, c:c + 1],
                                     accum_out=den[:, c:c + 1]).then_inc(ph.exp_done, 1)
                    u = k - 2
                    if ph.has(u):
                        i, kind, h, nb = ph.units[u]
                        act.wait_ge(ph.tp_done, u + 1)
                        if u >= 2:
                            act.wait_ge(ph.pv_done, u - 1)
                        rows_, w = (NSA_R * CMP_PAD, P) if kind == "c" else (P, P * nb)
                        a.activation(PTr[u % 2][0:rows_, 0:w], ps[3 + u % 2][0:rows_, 0:w], ACT.Copy)\
                            .then_inc(ph.pt_done, 1)
                    for r, i, fb in ph.rounds(k):
                        act.wait_ge(ph.ot_done, r + 1)
                        src = ps[7][:, 0:P * len(fb)].rearrange("p (k t) -> p k t", k=len(fb))
                        a.activation(ahi[:, fb[0]:fb[0] + len(fb), i * P:(i + 1) * P], src, ACT.Copy)\
                            .then_inc(ph.ot_hi, 1)

            attention(PA)
            act.wait_ge(h_done, NM)
            act.dma_start(gbc[:, :], g_m.to_broadcast([P, D])).then_inc(gain_full, 16)
            dense(KEY["out0"])
            for t in range(MT):
                q = NM + t
                act.wait_ge(xin_full[q % 2], 16 * (q // 2 + 1))
                act.wait_ge(PA.ot_done, 2 * NT)
                square(q, tok[:, q % 2, :])
            dense(KEY["out1"])
            for t in range(MT):
                norm_hi(NM + t, memhi, t)
            act.wait_ge(h_done, NM + MT)
            act.dma_start(gbc[:, :], g_x.to_broadcast([P, D])).then_inc(gain_full, 16)
            dense(KEY["out2"])
            dense(KEY["out3"])
            for t in range(NT):
                act.wait_ge(evac["dve"], evacs(of_piece[KEY["out3"]][t], "dve"))
                square(N2 + t, X[:, t, :])
                dense(KEY["mk0"] + t)
                if t:
                    norm_hi(N2 + t - 1, ahi, t - 1)
            norm_hi(N2 + NT - 1, ahi, NT - 1)
            act.wait_ge(h_done, N3)
            act.dma_start(gbc[:, :], g_f.to_broadcast([P, D])).then_inc(gain_full, 16)
            for n in range(KEY["mv0"], KEY["xo0"]):
                dense(n)
            attention(PX)
            for n in range(KEY["xo0"], ND):
                dense(n)
            act.wait_ge(zero_done, 1)
            act.dma_start(h3d[T:T + P, :], tok[:, 0, :]).then_inc(zero_out, 16)
            act.dma_start(xod[T:T + P, :], tok[:, 0, :]).then_inc(zero_out, 16)
            for t in range(NT):
                act.wait_ge(evac["dve"], evacs(of_piece[ND - 1][t], "dve"))
                if t >= 2:
                    act.wait_ge(h3_out[t - 2], 16)
                square(N3 + t, X[:, t, :])
                act.dma_start(xod[t * P:(t + 1) * P, :], X[:, t, :]).then_inc(xo_out, 16)
                act.wait_ge(h_done, N3 + t + 1)
                act.dma_start(h3d[t * P:(t + 1) * P, :], tok[:, 2 + (N3 + t) % 2, :]).then_inc(h3_out[t], 16)
                norm_hi(N3 + t, ahi, t)
            act.dma_start(gbc[:, :], g_o.rearrange("(a n) -> a n", a=1).to_broadcast([P, D])).then_inc(gain_full, 16)
            R = work[:, 0:2048]
            act.wait_ge(r_step, 1)
            a.activation(R[:, 96:112], R[:, 80:96], ACT.Exp).then_inc(r_exp, 1)
            act.wait_ge(r_step, 2)
            a.activation(R[:, 392:396], R[:, 388:392], ACT.Exp).then_inc(r_exp, 1)

            def xg_hi_out(n):
                for b in range(2):
                    act.wait_ge(xg_tp, n + b + 1)
                    a.activation(xghi[:, 4 * b:4 * b + 4, :], ps[2 + b][:, :].rearrange("p (k t) -> p k t", k=4),
                                 ACT.Copy).then_inc(xg_hi, 1)

            def silu(n_used, j):
                act.wait_ge(used, n_used)
                act.wait_ge(he_done, j)
                a.activation(sg, ps[0][:, :], ACT.Silu).then_inc(silu_done, 1)

            def he_hi_out(n):
                act.wait_ge(he_tp, n)
                a.activation(hehi, ps[6][:, :].rearrange("p (k t) -> p k t", k=KF), ACT.Copy).then_inc(he_hi, 1)

            def y_out_half(b, n_used):
                act.wait_ge(used, n_used)
                a.activation(tok[:, 2, 512 * b:512 * b + 512], ps[4 + b][:, :], ACT.Copy,
                             scale=yw[:, :]).then_inc(y_done, 1)

            split_expert(2)
            xg_hi_out(0)
            split_expert(3)
            split_expert(4)
            silu(2, 1)
            split_expert(5)
            split_expert(6)
            xg_hi_out(2)
            he_hi_out(1)
            act.wait_ge(route_done, 1)
            turns = act.value_load(etab[0:1, MAXCH:MAXCH + 1], min_val=NEXP - 2, max_val=MAXCH - 3)

            def turn(j, last):
                base = 6 * (j - 1) + 4
                split_expert(7, j)
                split_expert(8, j)
                silu(base + 2, j + 1)
                split_expert(9, j)
                split_expert(10, j)
                xg_hi_out(2 * j + 2)
                split_expert(11, j)
                act.wait_ge(yw_done, j)
                y_out_half(0, base + 5)
                if not last:
                    split_expert(12, j)
                y_out_half(1, base + 6)
                he_hi_out(j + 1)

            with act.Fori(1, turns + 1) as j:
                turn(j, False)
            turn(turns + 1, True)
            act.wait_ge(yw_done, turns + 2)
            y_out_half(0, 6 * turns + 11)
            y_out_half(1, 6 * turns + 12)
            for t in range(NT):
                q = N4 + t
                act.wait_ge(xin_full[q % 2], 16 * ((NT + MT) // 2 + t // 2 + 1))
                if t < 2:
                    act.wait_ge(adds_done, 1)
                else:
                    act.wait_ge(out_done[t - 2], 16)
                square(q, tok[:, q % 2, :])

        @block.vector
        def _(dve):
            v = nc.vector
            chain = [0]

            def mark(ins):
                chain[0] += 1
                ins.then_inc(dch, 1)
                return chain[0]

            def link(ins):
                dve.wait_ge(dch, mark(ins))

            link(v.memset(wpool[:, :, :], 0.0))
            link(v.memset(Vc[0:NSA_R * CMP_PAD, :, :], 0.0))
            v.memset(Kc[0:64, :, :], 0.0).then_inc(pad_done, 1)

            def split(n):
                dve.wait_ge(hi_done, n + 1)
                v.tensor_tensor(wlo[:, n % SPLIT, :], raw[:, n % RAW, :], whi[:, n % SPLIT, :].bitcast(F32),
                                ALU.subtract).then_inc(lo_done, 1)

            def split_expert(m, j=None):
                n = ND + m + 1
                dve.wait_ge(hi_done, n if j is None else 6 * (j - 1) + n)
                hi, lo = moe_split(m)
                v.tensor_tensor(lo, moe_raw(m), hi.bitcast(F32), ALU.subtract).then_inc(lo_done, 1)

            def norm(q, src):
                dve.wait_ge(ss_done, q + 1)
                v.tensor_scalar(stat[:, 1, q:q + 1], stat[:, 0, q:q + 1], 1.0 / D, EPS, ALU.mult, ALU.add)\
                    .then_inc(ms_done, 1)
                dve.wait_ge(rms_done, q + 1)
                v.scalar_tensor_tensor(tok[:, 2 + q % 2, :], src, stat[:, 2, q:q + 1], gbc[:, :],
                                       ALU.mult, ALU.mult).then_inc(h_done, 1)

            def norm_lo(q, dst, hi, t):
                for b in range(2):
                    dve.wait_ge(ntp_hi, 2 * q + b + 1)
                    src = ps[4 + 2 * (q % 2) + b][:, :].rearrange("p (k t) -> p k t", k=4)
                    sl = (slice(None), slice(4 * b, 4 * b + 4), slice(t * P, (t + 1) * P))
                    v.tensor_tensor(dst[sl], src, hi[sl].bitcast(F32), ALU.subtract).then_inc(ntp_lo, 1)

            def pool_tile(f, bank):
                v.tensor_copy(Ub[:, 16:UW], bank[:, :]).then_inc(evac["dve"], 1)
                dve.wait_ge(evac["dve"], f + 1)
                lo_w = POOL_WINDOWS[2 * f]
                src, dst = Ub, Sa
                width = 1
                spans = {}
                while width < POOL_WINDOWS[2 * f + 1]:
                    s = 2 * width - 1
                    link(v.tensor_tensor(dst[:, s:UW], src[:, s:UW], src[:, s - width:UW - width], ALU.add))
                    width *= 2
                    if width == lo_w:
                        emit_rows(f, 0, dst)
                    src, dst = dst, (Sb if dst is Sa else Sa)
                emit_rows(f, 1, src)

            def emit_rows(f, half_, s):
                r = slice(64 * half_, 64 * half_ + 64)
                link(v.tensor_tensor(pooled[r, f, 0:16], s[r, 16:32], corr[r, f, :], ALU.mult))
                link(v.scalar_tensor_tensor(pooled[r, f, 0:16], pooled[r, f, 0:16], invw[r, f, :],
                                            Ub[r, 16:32], ALU.mult, ALU.subtract))
                ins = v.scalar_tensor_tensor(pooled[r, f, 16:T], s[r, 32:UW], invw[r, f, :], Ub[r, 32:UW],
                                             ALU.mult, ALU.subtract)
                if half_:
                    ins.then_inc(pooled_done, 1)
                    dve.wait_ge(pooled_done, f + 1)

            def compress_blocks(kv):
                g_kcm = of_piece[KEY["fq1" if kv == 0 else "fk1"]][1]
                dve.wait_ge(evac["act"], evacs(g_kcm, "act"))
                if kv:
                    dve.wait_ge(fhi_done, 1)
                    dve.wait_ge(flo_done, 1)
                for g in range(NSA_G):
                    src = KG[kv][:, g, :]
                    a0 = src[:, 0:N_CMP * 16].rearrange("p (c j e) -> p j c e", j=8, e=2)[:, :, :, 0]
                    a1 = src[:, 16:16 + N_CMP * 16].rearrange("p (c j e) -> p j c e", j=8, e=2)[:, :, :, 0]
                    for b, s in enumerate((a0, a1)):
                        pe_b = pe2[:, kv, 8 * b:8 * b + 8].unsqueeze(2).to_broadcast([P, 8, N_CMP])
                        ins = v.tensor_tensor(Fb[:, 8 * b:8 * b + 8, g, :], s, pe_b, ALU.add)
                        if (g, b) == (1, 1):
                            ins.then_inc(f_done, 1)
                dve.wait_ge(fhi_done, kv + 1)
                v.tensor_tensor(flo[kv].rearrange("p j m -> p (j m)"), Fb.rearrange("p a b c -> p (a b c)"),
                                fhi[kv].rearrange("p j m -> p (j m)").bitcast(F32), ALU.subtract).then_inc(flo_done, 1)

            def evacuate(n):
                key = ORDER[n]
                for g in of_piece[n]:
                    _, kind, idx, c0, w, eng = groups[g]
                    if eng != "dve":
                        continue
                    dve.wait_ge(grp_done, g + 1)
                    b = ps[g % DRING]
                    if key == "pool":
                        pool_tile(idx, b)
                    else:
                        c = 256 * int(key[-1])
                        if key == "out0":
                            dve.wait_ge(x_in[idx], 16)
                        v.tensor_tensor(X[:, idx, c:c + 256], b[:, 0:256], X[:, idx, c:c + 256], ALU.add)\
                            .then_inc(evac["dve"], 1)

            def dense(n):
                evacuate(n)
                if n + SPLIT < ND:
                    split(n + SPLIT)
                else:
                    split_expert(n + SPLIT - ND)

            dve.wait_ge(half_set, 3)
            dve.wait_ge(gain_full, 16)
            for t in range(NT):
                norm(NX + t, tok[:, t % 2, :])
                if t == 0:
                    split(0)
                if t >= 1:
                    norm_lo(NX + t - 1, alo, ahi, t - 1)
            norm_lo(NX + NT - 1, alo, ahi, NT - 1)
            split(1)
            dve.wait_ge(sm_hi, 2)
            v.tensor_tensor(wsm_lo[:, :, :], wsm[:, :, :], wsm_hi[:, :, :].bitcast(F32), ALU.subtract).then_inc(sm_lo, 1)
            v.tensor_tensor(wrt_lo[:, :, :], wrt[:, :, :], wrt_hi[:, :, :].bitcast(F32), ALU.subtract).then_inc(sm_lo, 1)
            dense(0)
            dve.wait_ge(const_in, 16 * N_CONST)
            dve.wait_ge(small_mm, 1)
            z4 = ps[4][:, 0:NT * SMALL_W].rearrange("p (t c) -> p t c", t=NT)
            bb = bias24[:, :].unsqueeze(1).to_broadcast([P, NT, SMALL_W])
            link(v.tensor_tensor(zz[:, 0, :, :], z4, bb, ALU.add))
            link(v.tensor_scalar(zz[:, 1, :, :], zz[:, 0, :, :], -1.0, None, ALU.mult))
            link(v.tensor_tensor(zz[:, 1, :, 0:FOX_H], zz[:, 0, :, 0:FOX_H], zz[:, 1, :, 0:FOX_H], ALU.min))
            v.tensor_scalar(zz[:, 4, :, 0:FOX_H], zz[:, 0, :, 0:FOX_H], 0.0, None, ALU.min).then_inc(z_done, 1)
            dve.wait_ge(zexp_done, 2)
            dve.wait_ge(z_done, 1)
            v.tensor_tensor(zz[:, 4, :, 0:FOX_H], zz[:, 4, :, 0:FOX_H], zz[:, 3, :, 0:FOX_H], ALU.subtract)\
                .then_inc(lf_done, 1)
            link(v.tensor_scalar(zz[:, 5, :, FOX_H:], zz[:, 2, :, FOX_H:], 1.0, None, ALU.add))
            v.reciprocal(zz[:, 5, :, FOX_H:], zz[:, 5, :, FOX_H:]).then_inc(gate_done, 1)
            dense(1)
            compress_blocks(0)
            dense(2)
            dense(3)
            compress_blocks(1)
            dve.wait_ge(const2_in, 16 * N_CONST2)
            v.tensor_copy(bfc[:, :], bf_stage).then_inc(bf_done, 1)
            dve.wait_ge(bf_done, 1)
            dve.wait_ge(cum_mm, 1)
            dve.wait_ge(cumrow_in, 32)
            link(v.memset(Ub[:, 0:16], 0.0))
            link(v.memset(Sa[:, 0:16], 0.0))
            link(v.memset(Sb[:, 0:16], 0.0))
            for n in range(4, KEY["out0"]):
                dense(n)
            dve.wait_ge(kv2_mm, 2)
            for g in range(NSA_G):
                for r in range(NSA_R):
                    ins = v.tensor_copy(Vc[CMP_PAD * r:CMP_PAD * r + N_CMP, g, DH * r:DH * (r + 1)],
                                        ps[5][0:N_CMP, DH * g:DH * (g + 1)])
            ins.then_inc(vc_done, 1)
            HB = NSA_R * NT
            for b in range(2):
                dve.wait_ge(cs_done, b + 1)
                s3 = ps[6 + b][:, 0:HB * CMP_PAD].rearrange("p (i r c) -> p i r c", i=NT, c=CMP_PAD)
                p3 = Pc[:, :, NSA_R * b:NSA_R * (b + 1), :]
                m = cst[:, 0, HB * b:HB * (b + 1)].rearrange("p (i r) -> p i r", i=NT)
                link(v.tensor_reduce(m, s3, AX.X, ALU.max))
                link(v.tensor_scalar(m, m, -1e20, None, ALU.max))
                v.tensor_tensor(p3, s3, m.unsqueeze(3).to_broadcast([P, NT, NSA_R, CMP_PAD]), ALU.subtract)\
                    .then_inc(csub_done, 1)
            dve.wait_ge(cexp_done, 2)
            pall = Pc.rearrange("p a b c -> p (a b) c")
            link(v.tensor_reduce(cst[:, 1, :], pall, AX.X, ALU.add))
            link(v.tensor_scalar(cst[:, 2, :], cst[:, 1, :], 1e-30, None, ALU.max))
            link(v.reciprocal(cst[:, 3, :], cst[:, 2, :]))
            dve.wait_ge(gate_done, 1)
            gates = zz[:, 5, :, FOX_H:].rearrange("p t (h b) -> p t h b", b=3)
            link(v.tensor_tensor(cst[:, 4, :].rearrange("p (t h) -> p t h", t=NT),
                                 cst[:, 3, :].rearrange("p (t h) -> p t h", t=NT), gates[:, :, :, 0], ALU.mult))
            v.tensor_tensor(pall, pall, cst[:, 4, :].unsqueeze(2).to_broadcast([P, 2 * HB, CMP_PAD]), ALU.mult)\
                .then_inc(pc_done, 1)
            for f in range(2):
                dve.wait_ge(mix_hi, f + 1)
                v.scalar_tensor_tensor(alo[:, 3 + f, :], ps[4 + f][:, :], pscale[:, f, :],
                                       ahi[:, 3 + f, :].bitcast(F32), ALU.mult, ALU.subtract).then_inc(mix_lo, 1)

            def attention(ph):
                marks = {}
                for k in range(ph.steps):
                    if ph.score(k):
                        s = ph.sidx[k]
                        nk = P * ph.units[k][3]
                        dve.wait_ge(ph.scores_done, s + 1)
                        c = ph.col0 + s
                        v.tensor_reduce(nmax[:, c:c + 1], ps[s % 3][:, 0:nk], AX.X, ALU.max, negate=True)\
                            .then_inc(ph.max_done, 1)
                    u = k - 1
                    if ph.score(u):
                        s = ph.sidx[u]
                        c = ph.col0 + s
                        dve.wait_ge(ph.exp_done, s + 1)
                        marks[u] = mark(v.reciprocal(rden[:, c:c + 1], den[:, c:c + 1]))
                    u = k - 3
                    if ph.has(u):
                        i, kind, h, nb = ph.units[u]
                        c = ph.col0 + ph.sidx[u]
                        dve.wait_ge(ph.pv_done, u + 1)
                        ot = tok[:, 2 + i % 2, :]
                        if u % ph.per == 0 and i >= 2:
                            dve.wait_ge(ph.ot_done, 2 * (i - 1))
                        b = ps[5 + u % 2]
                        if kind == "c":
                            w = NSA_R * DH
                            c0 = FOX_W + POOL_W + h * w
                            v.tensor_copy(ot[:, c0:c0 + w], b[:, 0:w]).then_inc(ph.o_done, 1)
                        elif kind in "fx":
                            w = DH if kind == "f" else D // MEM_H
                            dve.wait_ge(dch, marks[u])
                            v.tensor_scalar(ot[:, h * w:h * w + w], b[:, 0:w], rden[:, c:c + 1], None, ALU.mult)\
                                .then_inc(ph.o_done, 1)
                        else:
                            c0 = FOX_W + POOL_W + h * DH
                            dve.wait_ge(dch, marks[("g", u)])
                            dve.wait_ge(ph.o_done, u)
                            v.scalar_tensor_tensor(ot[:, c0:c0 + DH], b[:, 0:DH], coef[:, c:c + 1], ot[:, c0:c0 + DH],
                                                   ALU.mult, ALU.add).then_inc(ph.o_done, 1)
                    u = k - 1
                    if ph.score(u) and ph.units[u][1] in "sw":
                        i, kind, h, nb = ph.units[u]
                        c = ph.col0 + ph.sidx[u]
                        gate = zz[:, 5, i, FOX_H + 3 * h + 1 + (kind == "w"):FOX_H + 3 * h + 2 + (kind == "w")]
                        dve.wait_ge(dch, marks[u])
                        marks[("g", u)] = mark(v.tensor_tensor(coef[:, c:c + 1], rden[:, c:c + 1], gate, ALU.mult))
                    for r, i, fb in ph.rounds(k):
                        dve.wait_ge(ph.ot_hi, r + 1)
                        src = ps[7][:, 0:P * len(fb)].rearrange("p (k t) -> p k t", k=len(fb))
                        sl = (slice(None), slice(fb[0], fb[0] + len(fb)), slice(i * P, (i + 1) * P))
                        v.tensor_tensor(alo[sl], src, ahi[sl].bitcast(F32), ALU.subtract).then_inc(ph.ot_lo, 1)

            attention(PA)
            dense(KEY["out0"])
            dve.wait_ge(gain_full, 32)
            for t in range(MT):
                norm(NM + t, tok[:, (NM + t) % 2, :])
            dense(KEY["out1"])
            for t in range(MT):
                norm_lo(NM + t, memlo, memhi, t)
            dense(KEY["out2"])
            dense(KEY["out3"])
            dve.wait_ge(gain_full, 48)
            for t in range(NT):
                norm(N2 + t, X[:, t, :])
                dense(KEY["mk0"] + t)
                if t:
                    norm_lo(N2 + t - 1, alo, ahi, t - 1)
            norm_lo(N2 + NT - 1, alo, ahi, NT - 1)
            for n in range(KEY["mv0"], KEY["xo0"]):
                dense(n)
            attention(PX)
            v.memset(tok[:, 0, :], 0.0).then_inc(zero_done, 1)
            for n in range(KEY["xo0"], ND):
                dense(n)
            dve.wait_ge(gain_full, 64)
            for t in range(NT):
                norm(N3 + t, X[:, t, :])
                norm_lo(N3 + t, alo, ahi, t)
            R = work[:, 0:2048]

            def r3(at, c, t=NT):
                return R[:, at:at + t * c].rearrange("p (t c) -> p t c", t=t)

            L = r3(0, ROUT_W)
            dve.wait_ge(route_mm, 1)
            link(v.tensor_tensor(L, ps[0][:, 0:NT * ROUT_W].rearrange("p (t c) -> p t c", t=NT),
                                 rbias[:, :].unsqueeze(1).to_broadcast([P, NT, ROUT_W]), ALU.add))
            Lc, Lf = L[:, :, 0:NGRP], L[:, :, NGRP:]
            sh, ex, cm = r3(80, 4), r3(96, 4), r3(112, 1)
            link(v.tensor_reduce(R[:, 112:116], Lc, AX.X, ALU.max))
            bc4 = [P, NT, 4]
            v.tensor_tensor(sh, Lc, cm.to_broadcast(bc4), ALU.subtract).then_inc(r_step, 1)

            def first_max(src, at, top):
                e, m, o = r3(at, 4), r3(at + 16, 1), r3(at + 20, 4)
                link(v.tensor_tensor(e, src, top.to_broadcast(bc4), ALU.is_equal))
                link(v.tensor_tensor(e, e, tiew[:, :].unsqueeze(1).to_broadcast(bc4), ALU.mult))
                link(v.tensor_reduce(R[:, at + 16:at + 20], e, AX.X, ALU.max))
                link(v.tensor_tensor(o, e, m.to_broadcast(bc4), ALU.is_equal))
                return o

            og = first_max(Lc, 120, cm)
            fm = R[:, 160:224].rearrange("p (t g e) -> p t g e", t=NT, g=NGRP)
            link(v.tensor_tensor(fm, Lf.rearrange("p t (g e) -> p t g e", g=NGRP),
                                 og.unsqueeze(3).to_broadcast([P, NT, NGRP, PER]), ALU.mult))
            f4 = r3(224, 4)
            link(v.tensor_reduce(f4, fm.rearrange("p t g e -> p t e g"), AX.X, ALU.add))
            m1 = r3(240, 1)
            link(v.tensor_reduce(R[:, 240:244], f4, AX.X, ALU.max))
            o1 = first_max(f4, 244, m1)
            f4b = r3(288, 4)
            link(v.scalar_tensor_tensor(f4b, o1, -1e30, f4, ALU.mult, ALU.add))
            m2 = r3(304, 1)
            link(v.tensor_reduce(R[:, 304:308], f4b, AX.X, ALU.max))
            o2 = first_max(f4b, 308, m2)
            v.tensor_tensor(R[:, 388:392], R[:, 304:308], R[:, 240:244], ALU.subtract).then_inc(r_step, 1)
            oh = [R[:, 400 + 64 * b:464 + 64 * b].rearrange("p (t g e) -> p t g e", t=NT, g=NGRP) for b in range(2)]
            for o, ok in zip(oh, (o1, o2)):
                link(v.tensor_tensor(o, og.unsqueeze(3).to_broadcast([P, NT, NGRP, PER]),
                                     ok.unsqueeze(2).to_broadcast([P, NT, NGRP, PER]), ALU.mult))
            ohb = work[:, 2048:2080].bitcast(BF16)
            v.tensor_tensor(ohb, R[:, 400:464], R[:, 464:528], ALU.add).then_inc(onehot_done, 1)
            dve.wait_ge(r_exp, 2)
            link(v.tensor_reduce(R[:, 540:544], ex, AX.X, ALU.add))
            link(v.tensor_scalar(R[:, 544:548], R[:, 392:396], 1.0, None, ALU.add))
            link(v.tensor_tensor(R[:, 540:544], R[:, 540:544], R[:, 544:548], ALU.mult))
            link(v.reciprocal(R[:, 548:552], R[:, 540:544]))
            lw = lst[:, :, 1:2].bitcast(F32).rearrange("p (k t) a -> p k (t a)", k=2)
            link(v.tensor_copy(lw[:, 0, :], R[:, 548:552]))
            link(v.tensor_tensor(lw[:, 1, :], R[:, 548:552], R[:, 392:396], ALU.mult))
            for b in range(2):
                link(v.tensor_copy(lst[:, NT * b:NT * (b + 1), 0], tokid))
            dve.wait_ge(rank_mm, 2)
            cnt = R[:, 560:576]
            nov = [R[:, 576 + 16 * b:592 + 16 * b] for b in range(2)]
            link(v.tensor_copy(cnt, ps[2][:, 0:NEXP]))
            link(v.tensor_scalar(nov[0], cnt, float(CHUNK), None, ALU.is_gt))
            for c in range(2, T // CHUNK):
                link(v.scalar_tensor_tensor(nov[0], cnt, float(CHUNK * c), nov[0], ALU.is_gt, ALU.add))
            link(v.tensor_copy(R[:, 620:636], nov[0]))
            cur = 0
            for s in (1, 2, 4, 8):
                link(v.tensor_copy(nov[1 - cur][:, 0:s], nov[cur][:, 0:s]))
                link(v.tensor_tensor(nov[1 - cur][:, s:], nov[cur][:, s:], nov[cur][:, 0:NEXP - s], ALU.add))
                cur = 1 - cur
            inc = nov[cur]
            exc = nov[1 - cur]
            link(v.tensor_tensor(exc, inc, R[:, 620:636], ALU.subtract))
            NO = MAXCH - NEXP
            cmpb = R[:, 700:700 + NO * NEXP].rearrange("p (i e) -> p i e", e=NEXP)
            link(v.tensor_tensor(cmpb, inc.unsqueeze(1).to_broadcast([P, NO, NEXP]),
                                 hgrid[:, 0:NO].unsqueeze(2).to_broadcast([P, NO, NEXP]), ALU.is_le))
            link(v.tensor_reduce(R[:, 640:640 + NO], cmpb, AX.X, ALU.add))
            link(v.tensor_scalar(R[:, 640:640 + NO], R[:, 640:640 + NO], float(NEXP - 1), None, ALU.min))
            link(v.tensor_copy(etab[:, 0:NEXP], eiota))
            link(v.tensor_copy(etab[:, NEXP:MAXCH], R[:, 640:640 + NO]))
            link(v.tensor_scalar(etab[:, MAXCH:MAXCH + 1], inc[:, NEXP - 1:NEXP], float(NEXP - 2), None, ALU.add))
            jump = R[:, 660:676]
            link(v.tensor_scalar(jump, exc, float(CHUNK), float(CHUNK * (NEXP - 1)), ALU.mult, ALU.add))
            link(v.scalar_tensor_tensor(jump, eiota, -float(CHUNK), jump, ALU.mult, ALU.add))
            rank = R[:, 900:964].rearrange("p (t e) -> p t e", t=NT)
            slot = R[:, 964:1028].rearrange("p (t e) -> p t e", t=NT)
            tmp = R[:, 1028:1092].rearrange("p (t e) -> p t e", t=NT)
            link(v.tensor_copy(rank, ps[1][:, 0:NT * NEXP].rearrange("p (t e) -> p t e", t=NT)))
            link(v.tensor_scalar(tmp, rank, float(CHUNK), None, ALU.is_ge))
            b16 = [P, NT, NEXP]
            link(v.tensor_tensor(tmp, tmp, jump.unsqueeze(1).to_broadcast(b16), ALU.mult))
            link(v.tensor_tensor(slot, rank, tmp, ALU.add))
            link(v.scalar_tensor_tensor(slot, eiota.unsqueeze(1).to_broadcast(b16), float(CHUNK), slot,
                                        ALU.mult, ALU.add))
            for b in range(2):
                link(v.tensor_tensor(tmp, slot, R[:, 400 + 64 * b:464 + 64 * b].rearrange("p (t e) -> p t e", t=NT),
                                     ALU.mult))
                link(v.tensor_reduce(R[:, 1100 + 4 * b:1104 + 4 * b], tmp, AX.X, ALU.add))
            v.tensor_copy(posi[:, :], R[:, 1100:1108]).then_inc(route_done, 1)

            v.memset(sg, 0.0).then_inc(he_done, 1)
            dve.wait_ge(he_done, 1)

            def xg_lo_out(n):
                for b in range(2):
                    dve.wait_ge(xg_hi, n + b + 1)
                    v.tensor_tensor(xglo[:, 4 * b:4 * b + 4, :], ps[2 + b][:, :].rearrange("p (k t) -> p k t", k=4),
                                    xghi[:, 4 * b:4 * b + 4, :].bitcast(F32), ALU.subtract).then_inc(xg_lo, 1)

            def gated(n_silu, n_used, n_tp=None):
                dve.wait_ge(silu_done, n_silu)
                dve.wait_ge(used, n_used)
                if n_tp is not None:
                    dve.wait_ge(he_tp, n_tp)
                v.tensor_tensor(he, sg, ps[1][:, :], ALU.mult).then_inc(he_done, 1)

            def he_lo_out(n):
                dve.wait_ge(he_hi, n)
                v.tensor_tensor(helo, ps[6][:, :].rearrange("p (k t) -> p k t", k=KF), hehi.bitcast(F32),
                                ALU.subtract).then_inc(he_lo, 1)

            split_expert(2)
            xg_lo_out(0)
            split_expert(3)
            split_expert(4)
            split_expert(5)
            split_expert(6)
            gated(1, 4)
            xg_lo_out(2)
            he_lo_out(1)
            dve.wait_ge(route_done, 1)
            turns = dve.value_load(etab[0:1, MAXCH:MAXCH + 1], min_val=NEXP - 2, max_val=MAXCH - 3)

            def turn(j, last):
                for m in (7, 8, 9, 10):
                    split_expert(m, j)
                gated(j + 1, 6 * (j - 1) + 8, j)
                xg_lo_out(2 * j + 2)
                split_expert(11, j)
                if not last:
                    split_expert(12, j)
                he_lo_out(j + 1)

            with dve.Fori(1, turns + 1) as j:
                turn(j, False)
            turn(turns + 1, True)
            dve.wait_ge(gain_full, 80)
            for t in range(NT):
                norm(N4 + t, tok[:, (N4 + t) % 2, :])

        @block.tensor
        def _(pe):
            mm = nc.tensor.matmul

            def three(out_, ahi_, alo_, bhi_, blo_, first, last):
                mm(out_, ahi_, bhi_, start=first, stop=False)
                mm(out_, ahi_, blo_, start=False, stop=False)
                return mm(out_, alo_, bhi_, start=False, stop=last)

            def dense(n):
                pe.wait_ge(lo_done, n + 1)
                hi = whi[:, n % SPLIT, :].rearrange("p (k n) -> p k n", k=KD)
                lo = wlo[:, n % SPLIT, :].rearrange("p (k n) -> p k n", k=KD)
                mem = ORDER[n][:2] in ("mk", "mv")
                xh, xl, nt = (memhi, memlo, MEM) if mem else (ahi, alo, T)
                for g in of_piece[n]:
                    _, kind, idx, c0, w, eng = groups[g]
                    if kind == "C":
                        kv, b = idx // 2, idx % 2
                        if b == 0:
                            pe.wait_ge(flo_done, kv + 1)
                            if kv:
                                pe.wait_ge(gelu_done, 1)
                        for hb in range(2):
                            for j in range(8):
                                ins = three(ps[6 + hb][:, 0:2 * N_CMP],
                                            hi[:, j, P * hb:P * hb + P], lo[:, j, P * hb:P * hb + P],
                                            fhi[kv][:, 8 * b + j, :], flo[kv][:, 8 * b + j, :],
                                            b == 0 and j == 0, b == 1 and j == 7)
                        ins.then_inc(grp_done, 1)
                        continue
                    if g >= DRING and groups[g - DRING][5]:
                        e = groups[g - DRING][5]
                        pe.wait_ge(evac[e], evacs(g - DRING, e))
                    bank = ps[g % DRING]
                    for k in range(KD):
                        if kind == "F":
                            wc = slice(c0, c0 + P)
                            ins = three(bank[:, 0:nt], hi[:, k, wc], lo[:, k, wc], xh[:, k, :], xl[:, k, :],
                                        k == 0, k == KD - 1)
                        else:
                            tc = slice(idx * P, (idx + 1) * P)
                            ins = three(bank[:, 0:w], xh[:, k, tc], xl[:, k, tc], hi[:, k, c0:c0 + w],
                                        lo[:, k, c0:c0 + w], k == 0, k == KD - 1)
                    ins.then_inc(grp_done, 1)

            def norm_transposes(q):
                pe.wait_ge(h_done, q + 1)
                if q >= 2:
                    pe.wait_ge(ntp_lo, 2 * (q - 1))
                for b in range(2):
                    for m in range(4):
                        c = (4 * b + m) * P
                        ins = nc.tensor.transpose(ps[4 + 2 * (q % 2) + b][:, m * P:(m + 1) * P],
                                                  tok[:, 2 + q % 2, c:c + P], ident[:, :])
                    ins.then_inc(ntp_done, 1)

            pe.wait_ge(ident_in, 16)
            for t in range(NT):
                norm_transposes(NX + t)
            pe.wait_ge(ntp_lo, 2 * NT)
            dense(0)
            pe.wait_ge(sm_lo, 1)
            for t in range(NT):
                for k in range(KD):
                    tc = slice(t * P, (t + 1) * P)
                    ins = three(ps[4][:, t * SMALL_W:(t + 1) * SMALL_W], ahi[:, k, tc], alo[:, k, tc],
                                wsm_hi[:, k, :], wsm_lo[:, k, :], k == 0, k == KD - 1)
            ins.then_inc(small_mm, 1)
            dense(1)
            pe.wait_ge(lf_done, 1)
            pe.wait_ge(const_in, 16 * N_CONST)
            for t in range(NT):
                ins = mm(ps[5][0:FOX_H, t * P:T], zz[:, 4, t, 0:FOX_H], tri[:, 0:T - t * P],
                         start=(t == 0), stop=(t == NT - 1))
            ins.then_inc(cum_mm, 1)
            for n in range(2, KEY["out0"]):
                dense(n)
                if ORDER[n] == "nq1":
                    pe.wait_ge(gelu_done, 2)
                    pe.wait_ge(const2_in, 16 * N_CONST2)
                    for hb in range(2):
                        ins = mm(ps[4][0:DH, 0:2 * N_CMP], w2[:, 0, hb, :], gT[:, 0, hb, :],
                                 start=(hb == 0), stop=(hb == 1))
                    ins.then_inc(kv2_mm, 1)
                    for g in range(NSA_G):
                        for hb in range(2):
                            ins = mm(ps[5][0:N_CMP, DH * g:DH * (g + 1)], gT[:, 1, hb, N_CMP * g:N_CMP * (g + 1)],
                                     w2[:, 1, hb, :], start=(hb == 0), stop=(hb == 1))
                    ins.then_inc(kv2_mm, 1)
            pe.wait_ge(kc_done, 1)
            pe.wait_ge(bf_done, 1)
            pe.wait_ge(rows_in, 16 * 6)
            for b in range(2):
                w = NSA_R * CMP_PAD
                mm(ps[6 + b][:, 0:NT * w].rearrange("p (i r c) -> p i r c", i=NT, r=NSA_R), identb,
                   maskc.rearrange("p (i c) -> p i c", i=NT).unsqueeze(2).to_broadcast([P, NT, NSA_R, CMP_PAD]),
                   start=True, stop=False)
                for r in range(NSA_R):
                    for i in range(NT):
                        c0 = w * i + CMP_PAD * r
                        ins = mm(ps[6 + b][:, c0:c0 + CMP_PAD], Qn[0:66, NSA_R * b + r, i * P:(i + 1) * P],
                                 Kc[0:66, b, :], start=False, stop=(r == NSA_R - 1 and i == NT - 1))
                ins.then_inc(cs_done, 1)
            pe.wait_ge(vc_done, 1)
            pe.wait_ge(pooled_done, 2)
            for f in range(2):
                mm(ps[4 + f][:, :], wpool[:, f, :], pooled[:, f, :], start=True, stop=True).then_inc(mix_mm, 1)

            def attention(ph):
                for k in range(ph.steps):
                    if ph.score(k):
                        i, kind, h, nb = ph.units[k]
                        s = ph.sidx[k]
                        bank = ps[s % 3]
                        if s >= 3:
                            pe.wait_ge(ph.exp_done, s - 2)
                        qc = slice(i * P, (i + 1) * P)
                        if kind == "x":
                            for e in range(2):
                                ins = mm(bank[:, 0:MEM], QTx[:, 2 * h + e, qc], KTm[:, 2 * h + e, :],
                                         start=(e == 0), stop=(e == 1))
                        else:
                            q = (Qf if kind == "f" else Qn)[0:66, h, qc]
                            kk = {"f": Kf, "s": Ks, "w": Kw}[kind][0:66, h if kind == "f" else h // NSA_R, 0:P * nb]
                            mm(bank[:, 0:P * nb], q, kk, start=True, stop=False)
                            ins = mm(bank[:, P * i:P * nb], identb, maskb, start=False, stop=True)
                        ins.then_inc(ph.scores_done, 1)
                    u = k - 2
                    if ph.has(u):
                        i, kind, h, nb = ph.units[u]
                        bank = ps[3 + u % 2]
                        if u >= 2:
                            pe.wait_ge(ph.pt_done, u - 1)
                        if kind == "c":
                            ins = nc.tensor.transpose(bank[0:NSA_R * CMP_PAD, 0:P],
                                                      Pc[:, i, NSA_R * h:NSA_R * (h + 1), :].rearrange("p r c -> p (r c)"),
                                                      ident[:, :])
                        else:
                            s = ph.sidx[u]
                            pe.wait_ge(ph.exp_done, s + 1)
                            for b in range(nb):
                                ins = nc.tensor.transpose(bank[:, P * b:P * (b + 1)], Pr[s % 3][:, P * b:P * (b + 1)],
                                                          ident[:, :])
                        ins.then_inc(ph.tp_done, 1)
                    u = k - 3
                    if ph.has(u):
                        i, kind, h, nb = ph.units[u]
                        bank = ps[5 + u % 2]
                        pt = PTr[u % 2]
                        pe.wait_ge(ph.pt_done, u + 1)
                        if u >= 2:
                            pe.wait_ge(ph.o_done, u - 1)
                        if kind == "c":
                            rws = NSA_R * CMP_PAD
                            ins = mm(bank[:, 0:NSA_R * DH], pt[0:rws, 0:P], Vc[0:rws, h, :], start=True, stop=True)
                        else:
                            w = D // MEM_H if kind == "x" else DH
                            for b in range(nb):
                                if kind == "x":
                                    val = Vm[:, b, w * h:w * (h + 1)]
                                elif kind == "f":
                                    val = Vf[:, b, w * h:w * (h + 1)]
                                else:
                                    val = (Vs if kind == "s" else Vw)[:, b, DH * (h // NSA_R):DH * (h // NSA_R) + DH]
                                ins = mm(bank[:, 0:w], pt[:, P * b:P * (b + 1)], val, start=(b == 0), stop=(b == nb - 1))
                        ins.then_inc(ph.pv_done, 1)
                    for r, i, fb in ph.rounds(k):
                        pe.wait_ge(ph.o_done, ph.per * (i + 1))
                        if r:
                            pe.wait_ge(ph.ot_lo, r)
                        for m, f in enumerate(fb):
                            ins = nc.tensor.transpose(ps[7][:, m * P:(m + 1) * P], tok[:, 2 + i % 2, f * P:(f + 1) * P],
                                                      ident[:, :])
                        ins.then_inc(ph.ot_done, 1)

            pe.wait_ge(evac["act"], evacs(of_piece[KEY["out0"]][0] - 1, "act"))
            pe.wait_ge(evac["dve"], evacs(of_piece[KEY["out0"]][0] - 1, "dve"))
            pe.wait_ge(mix_lo, 2)
            pe.wait_ge(pc_done, 1)
            pe.wait_ge(cumrow_in, 32)
            attention(PA)
            pe.wait_ge(PA.ot_lo, 2 * NT)
            dense(KEY["out0"])
            dense(KEY["out1"])
            for t in range(MT):
                norm_transposes(NM + t)
            dense(KEY["out2"])
            dense(KEY["out3"])
            pe.wait_ge(ntp_lo, 2 * (NM + MT))
            for t in range(NT):
                dense(KEY["mk0"] + t)
                norm_transposes(N2 + t)
            pe.wait_ge(ntp_lo, 2 * N3)
            for n in range(KEY["mv0"], KEY["xo0"]):
                dense(n)
            pe.wait_ge(evac["act"], evacs(of_piece[KEY["xo0"]][0] - 1, "act"))
            attention(PX)
            pe.wait_ge(PX.ot_lo, 2 * NT)
            for n in range(KEY["xo0"], ND):
                dense(n)
            for t in range(NT):
                norm_transposes(N3 + t)
            pe.wait_ge(ntp_lo, 2 * N4)
            pe.wait_ge(sm_lo, 2)
            pe.wait_ge(evac["dve"], evacs(len(groups) - 1, "dve"))
            for t in range(NT):
                for k in range(KD):
                    tc = slice(t * P, (t + 1) * P)
                    ins = three(ps[0][:, t * ROUT_W:(t + 1) * ROUT_W], ahi[:, k, tc], alo[:, k, tc],
                                wrt_hi[:, k, :], wrt_lo[:, k, :], k == 0, k == KD - 1)
            ins.then_inc(route_mm, 1)
            pe.wait_ge(onehot_done, 1)
            ohb = work[:, 2048:2080].bitcast(BF16).rearrange("p (t e) -> p t e", t=NT)
            for t in range(NT):
                for s in range(t + 1):
                    ins = mm(ps[1][:, NEXP * t:NEXP * (t + 1)], ones if s < t else sut, ohb[:, s, :],
                             start=(s == 0), stop=(s == t))
            ins.then_inc(rank_mm, 1)
            for s in range(NT):
                ins = mm(ps[2][:, 0:NEXP], ones, ohb[:, s, :], start=(s == 0), stop=(s == NT - 1))
            ins.then_inc(rank_mm, 1)
            pe.wait_ge(route_done, 1)

            def in_piece(bank, m, half_):
                hi, lo = (x.rearrange("p (k f) -> p k f", k=KF) for x in moe_split(m))
                for k in range(KF):
                    kk = KF * half_ + k
                    ins = three(bank[:, :], xghi[:, kk, :], xglo[:, kk, :], hi[:, k, :], lo[:, k, :],
                                kk == 0, kk == KD - 1)
                ins.then_inc(used, 1)

            def down_piece(bank, m):
                hi, lo = (x.rearrange("p (k f) -> p k f", k=KF) for x in moe_split(m))
                for k in range(KF):
                    ins = three(bank[:, :], hehi[:, k, :], helo[:, k, :], hi[:, k, :], lo[:, k, :],
                                k == 0, k == KF - 1)
                ins.then_inc(used, 1)

            def xg_transposes():
                for b in range(2):
                    for m in range(4):
                        c = (4 * b + m) * P
                        ins = nc.tensor.transpose(ps[2 + b][:, m * P:(m + 1) * P], tok[:, 0, c:c + P], ident[:, :])
                    ins.then_inc(xg_tp, 1)

            def he_transposes():
                for m in range(KF):
                    ins = nc.tensor.transpose(ps[6][:, m * P:(m + 1) * P], he[:, m * P:(m + 1) * P], ident[:, :])
                ins.then_inc(he_tp, 1)

            pe.wait_ge(xg_in, 16)
            xg_transposes()
            pe.wait_ge(xg_lo, 2)
            for m in range(4):
                pe.wait_ge(lo_done, ND + m + 1)
                in_piece(ps[m // 2], m, m % 2)
            pe.wait_ge(xg_in, 32)
            xg_transposes()
            pe.wait_ge(he_done, 2)
            he_transposes()
            turns = pe.value_load(etab[0:1, MAXCH:MAXCH + 1], min_val=NEXP - 2, max_val=MAXCH - 3)
            with pe.Fori(1, turns + 2) as j:
                n0 = 6 * (j - 1) + (NMP + 1)
                pe.wait_ge(xg_lo, 2 * j + 2)
                pe.wait_ge(silu_done, j)
                for m in range(2):
                    pe.wait_ge(lo_done, n0 + m)
                    in_piece(ps[0], 4 + m, m)
                pe.wait_ge(he_done, j + 1)
                for m in range(2):
                    pe.wait_ge(lo_done, n0 + 2 + m)
                    in_piece(ps[1], 6 + m, m)
                pe.wait_ge(xg_in, 16 * j + 32)
                xg_transposes()
                pe.wait_ge(he_lo, j)
                for m in range(2):
                    pe.wait_ge(lo_done, n0 + 4 + m)
                    down_piece(ps[4 + m], 8 + m)
                pe.wait_ge(he_done, j + 2)
                he_transposes()
            pe.wait_ge(he_lo, turns + 2)
            for m in range(2):
                pe.wait_ge(lo_done, 6 * turns + (NMP + 7 + m))
                down_piece(ps[4 + m], 10 + m)


_INS = ["x", "mem", "mix_norm_g", "w_in", "fox_forget_b", "pool_w", "cmp_w1_k", "cmp_w2_k", "cmp_w1_v",
        "cmp_w2_v", "nsa_gate_b", "w_out", "xattn_norm_g", "mem_norm_g", "xattn_wq", "xattn_wk", "xattn_wv",
        "xattn_wo", "ffn_norm_g", "router_coarse_w", "router_coarse_b", "router_fine_w", "router_fine_b",
        "exp_w_gate", "exp_w_up", "exp_w_down", "final_norm_g"]


def constants():
    import numpy as np
    f = np.float32
    i = np.arange(P)
    neg = f(-1e30)
    c_end = np.arange(CMP_PAD) * CMP_STRIDE + CMP_LEN - 1
    tok_ = np.arange(NT)[None, :] * P + i[:, None]
    maskc = np.where(tok_[:, :, None] >= c_end[None, None, :], f(0), neg)
    bf = np.concatenate([np.eye(P), np.where(i[None, :] <= i[:, None], 0, neg), maskc.reshape(P, -1),
                         i[:, None] < i[None, :], np.ones((P, P))], axis=1).astype(f)
    pool = np.zeros((P, 2, 17), f)
    for g, w in enumerate(POOL_WINDOWS):
        r = slice(64 * (g % 2), 64 * (g % 2) + 64)
        pool[r, g // 2, 0] = 1.0 / w
        pool[r, g // 2, 1:17] = w / np.minimum(np.arange(16) + 1, w)
    slopes = np.exp2(f(-8.0) * np.arange(1, NSA_H + 1, dtype=f) / f(NSA_H)).astype(f)
    t = np.arange(T, dtype=f)
    qrows = np.stack([-slopes[:, None] * t[None, :], np.repeat(slopes[:, None], T, 1)]).astype(f)
    krows = np.stack([np.ones((NSA_G, T)), np.repeat(t[None], NSA_G, 0)]).astype(f)
    crows = np.stack([np.ones((NSA_G, CMP_PAD)), np.repeat(c_end[None], NSA_G, 0)]).astype(f)
    row = np.concatenate([np.arange(MAXCH), [4, 3, 2, 1], np.arange(NEXP)]).astype(f)
    tabs = np.concatenate([np.repeat(row[None], P, 0), tok_.astype(f)], axis=1).astype(f)
    lst = np.stack([T + np.arange((MAXCH + 1) * P) % P, np.zeros((MAXCH + 1) * P)], axis=1).astype(np.int32)
    return {"ident": np.eye(P, dtype=f), "tri": (np.arange(T)[None, :] >= i[:, None]).astype(f), "bf": bf,
            "pool": pool, "tabs": tabs, "qrows": qrows, "krows": krows, "crows": crows,
            "ones": np.ones((1, FOX_H, T), f), "list": lst}


def kernel(**inputs):
    import numpy as _np
    import concourse.bacc as _bacc
    from concourse.bass_utils import run_bass_kernel_spmd as _run

    nc = _bacc.Bacc("TRN2", target_bir_lowering=False, num_devices=1)
    arrays = {}

    def give(name, a):
        a = _np.ascontiguousarray(a)
        arrays[name] = a
        return nc.dram_tensor(name, a.shape, mybir.dt.from_np(a.dtype), kind="ExternalInput").ap()

    A = {n: give(f"in_{n}", _np.asarray(inputs[n])) for n in _INS}
    for c in "kv":
        pe = _np.asarray(inputs[f"cmp_pe_{c}"])[0].reshape(16, 2, DH).transpose(1, 2, 0).reshape(P, 16)
        A[f"pe_{c}"] = give(f"in_pe_{c}", pe)
    A["pscale"] = give("in_pscale", _np.asarray(inputs["pool_scale"])[0].reshape(2, P).T)
    C = {n: give(f"c_{n}", a) for n, a in constants().items()}
    out = nc.dram_tensor("out_0", (1, T, D), F32, kind="ExternalOutput").ap()
    build(nc, A, C, out)
    r = _run(nc, [arrays], core_ids=[0])
    return r.results[0]["out_0"]
```

```python
import concourse.bass as bass
from concourse import mybir
from contextlib import ExitStack

F32 = mybir.dt.float32
F32R = mybir.dt.float32r
BF16 = mybir.dt.bfloat16
I32 = mybir.dt.int32
ALU = mybir.AluOpType
ACT = mybir.ActivationFunctionType
AX = mybir.AxisListType

P = 128
D = 1024
KD = D // P
T = 512
NT = T // P
DH = 64
FOX_H = 6
NSA_H = 6
NSA_G = 2
NSA_R = NSA_H // NSA_G
FOX_W = FOX_H * DH
POOL_W = 256
POOL_WINDOWS = (2, 4, 8, 16)
NSA_W = NSA_H * DH
KV_W = NSA_G * DH
SMALL_W = FOX_H + 3 * NSA_H
CMP_LEN, CMP_STRIDE = 32, 16
N_CMP = T // CMP_STRIDE - 1
CMP_PAD = 32
CMP_HID = 256
MEM = 256
MT = MEM // P
MEM_H = 4
NEXP = 16
NGRP = 4
PER = 4
FF = 512
KF = FF // P
EPS = 1e-6
ROUT_W = NGRP + NEXP

PIECE = 2048
RAW = 3
SPLIT = 2
MRAW, MSPLIT = 6, 3
DRING = 4
CHUNK = 96
N_CONST, N_CONST2 = 5, 12
MAXCH = NEXP + (2 * T) // CHUNK + 1
NLIST = MAXCH + 1


def offsets():
    names = ["fq", "fk", "fv", "ff", "pool", "nq", "kcm", "vcm", "ksl", "vsl", "kwn", "vwn", "gate"]
    widths = [FOX_W, FOX_W, FOX_W, FOX_H, POOL_W, NSA_W] + [KV_W] * 6 + [3 * NSA_H]
    at, out = 0, {}
    for n, w in zip(names, widths):
        out[n] = at
        at += w
    return out


def build(nc, A, C, out):
    O = offsets()
    with ExitStack() as ctx:
        def sb(name, shape, dt=F32):
            return ctx.enter_context(nc.sbuf_tensor(name, shape, dt))

        def sem(name):
            return ctx.enter_context(nc.semaphore(name))

        def dram(name, shape, dt=F32):
            return nc.dram_tensor(name, shape, dt, kind="Internal").ap()

        raw = sb("raw", [P, RAW, PIECE])
        whi = sb("whi", [P, SPLIT, PIECE], F32R)
        wlo = sb("wlo", [P, SPLIT, PIECE], F32R)
        ahi = sb("ahi", [P, KD, T], F32R)
        alo = sb("alo", [P, KD, T], F32R)
        mhi = sb("mhi", [P, KD * MEM], F32R)
        mlo = sb("mlo", [P, KD * MEM], F32R)
        arena = sb("arena", [P, 15040])
        gbc = sb("gbc", [P, D])
        tok = sb("tok", [P, 4, D])
        work = sb("work", [P, 2624])
        ident = sb("ident", [P, P])
        bfc = sb("bfc", [P, 5 * P], BF16)
        wsm_hi = sb("wsm_hi", [P, KD, SMALL_W], F32R)
        wsm_lo = sb("wsm_lo", [P, KD, SMALL_W], F32R)
        wrt_hi = sb("wrt_hi", [P, KD, ROUT_W], F32R)
        wrt_lo = sb("wrt_lo", [P, KD, ROUT_W], F32R)
        w2 = sb("w2", [P, 2, 2, DH])
        pe2 = sb("pe2", [P, 2, 16])
        wpool = sb("wpool", [P, 2, P])
        gT = sb("gT", [P, 2, 2, 2 * N_CMP])
        pcon = sb("pcon", [P, 2, 17])
        pscale_t = sb("pscale_t", [P, 2])
        bias24 = sb("bias24", [P, SMALL_W])
        rbias = sb("rbias", [P, ROUT_W])
        half = sb("half", [P, 1])
        stat = sb("stat", [P, 3, 20])
        zz = sb("zz", [P, 6, NT, SMALL_W])
        nmax = sb("nmax", [P, 96])
        den = sb("den", [P, 96])
        rden = sb("rden", [P, 96])
        coef = sb("coef", [P, 96])
        cst = sb("cst", [P, 5, 24])
        spare = sb("spare", [P, 2])
        zeroi = sb("zeroi", [P, 1], I32)
        ltok = sb("ltok", [P, NLIST], I32)
        lwt = sb("lwt", [P, NLIST])
        xidx = sb("xidx", [P, 1], I32)
        yidx = sb("yidx", [P, 1], I32)
        yw = sb("yw", [P, 1])
        etab = sb("etab", [P, MAXCH + 1], I32)
        tabs = sb("tabs", [P, MAXCH + 4 + NEXP + NT + NLIST + 2 + CHUNK])
        ps = [ctx.enter_context(nc.psum_tensor(f"ps{i}", [P, 512], F32)) for i in range(8)]

        h3d = dram("h3d", [T + P, D])
        xod = dram("xod", [T + P, D])

        def carve(at, *shape):
            n = 1
            for s in shape:
                n *= s
            ap = arena[:, at:at + n]
            if len(shape) == 1:
                return ap, at + n
            names = "abc"[:len(shape)]
            spec = f"p ({' '.join(names)}) -> p {' '.join(names)}"
            return ap.rearrange(spec, **{k: s for k, s in zip(names, shape)}), at + n

        Qf, at = carve(0, FOX_H, T)
        Kf, at = carve(at, FOX_H, T)
        Qn, at = carve(at, NSA_H, T)
        Ks, at = carve(at, NSA_G, T)
        Kw, at = carve(at, NSA_G, T)
        qk_end = at
        Vf, at = carve(at, NT, FOX_W)
        vs_at = at
        Vs, at = carve(at, NT, KV_W)
        Vw, at = carve(at, NT, KV_W)
        Fb, _ = carve(vs_at, 16, NSA_G, N_CMP)
        Kc, at = carve(at, NSA_G, CMP_PAD)
        Vc, at = carve(at, NSA_G, NSA_R * DH)
        Pc, at = carve(at, NT, NSA_H, CMP_PAD)
        assert at <= 15040
        X, at = carve(0, NT, D)
        QTx, at = carve(at, KD, T)
        KTm, at = carve(at, KD, MEM)
        Vm, at = carve(at, MT, D)
        assert at <= 15040

        raw_x, at = carve(NT * D, MRAW - RAW, PIECE)
        assert at <= NT * D + KD * (T + MEM)

        KG = [tok[:, b, :].rearrange("p (g t) -> p g t", g=NSA_G) for b in range(2)]
        Pr = [work[:, 512 * b:512 * b + 512] for b in range(3)] + [tok[:, 0, 0:512]]
        PTr = [work[:, 1536 + 512 * b:2048 + 512 * b] for b in range(2)] + [tok[:, 0, 512:1024]]
        tri = work[:, 0:T]
        gtok = work[0:2 * N_CMP, 0:2 * CMP_HID].rearrange("p (k n) -> p k n", k=2)
        wsm = work[:, 1800:1800 + KD * SMALL_W].rearrange("p (k c) -> p k c", k=KD)
        wrt = work[:, 2000:2000 + KD * ROUT_W].rearrange("p (k c) -> p k c", k=KD)
        zT = work[0:SMALL_W, 1280:1280 + T]
        rT = work[0:ROUT_W, 2080:2080 + T]
        UW = T + 16
        bf_stage = work[:, 640:640 + 5 * P]
        cumr = work[0:FOX_H, 1600:1600 + 2 * T].rearrange("p (b t) -> p b t", b=2)
        Ub, Sa, Sb = (work[:, UW * b:UW * (b + 1)] for b in range(3))
        pooled = work[:, 3 * UW:3 * UW + 2 * T].rearrange("p (f t) -> p f t", f=2)
        identb, maskb, maskc, sut, ones = (bfc[:, P * b:P * (b + 1)] for b in range(5))
        invw, corr, pscale = pcon[:, :, 0:1], pcon[:, :, 1:17], pscale_t[:, :].unsqueeze(2)
        fhi = [mhi[:, 992 * b:992 * (b + 1)].rearrange("p (j m) -> p j m", j=16) for b in range(2)]
        flo = [mlo[:, 992 * b:992 * (b + 1)].rearrange("p (j m) -> p j m", j=16) for b in range(2)]
        memhi = mhi[:, :].rearrange("p (k t) -> p k t", k=KD)
        memlo = mlo[:, :].rearrange("p (k t) -> p k t", k=KD)
        xghi = mhi[:, 0:KD * CHUNK].rearrange("p (k t) -> p k t", k=KD)
        xglo = mlo[:, 0:KD * CHUNK].rearrange("p (k t) -> p k t", k=KD)
        hehi = mhi[:, KD * CHUNK:KD * CHUNK + KF * CHUNK].rearrange("p (k t) -> p k t", k=KF)
        helo = mlo[:, KD * CHUNK:KD * CHUNK + KF * CHUNK].rearrange("p (k t) -> p k t", k=KF)
        sg, he = work[0:CHUNK, 0:FF], work[0:CHUNK, FF:2 * FF]
        at, cut = 0, []
        for w in (MAXCH, 4, NEXP, NT, NLIST + 1, 1, CHUNK):
            cut.append(tabs[:, at:at + w])
            at += w
        hgrid, tiew, eiota, tokid, cgrid, dummy, siota = cut

        def cols(w, c0, n):
            return w[:, c0:c0 + n].rearrange("(k p) n -> p k n", p=P)

        win, wout = A["w_in"][0], A["w_out"][0]
        wq, wk, wv, wo = (A[f"xattn_w{c}"][0] for c in "qkvo")
        pieces = []
        groups = []
        KEY = {}

        def piece(key, loads, grps):
            KEY[key] = len(pieces)
            for kind, idx, c0, n, eng in grps:
                groups.append((len(pieces), kind, idx, c0, n, eng))
            pieces.append(loads)

        def two(key, w, c0, eng="act"):
            piece(key, [(0, cols(w, c0, 256))], [("F", f, f * P, P, eng) for f in range(2)])

        def pair(key, w, c0, c1):
            piece(key, [(0, cols(w, c0, P)), (P, cols(w, c1, P))], [("F", f, f * P, P, "act") for f in range(2)])

        two("fq0", win, O["fq"])
        pair("fq1", win, O["fq"] + 256, O["kcm"])
        two("fk0", win, O["fk"])
        pair("fk1", win, O["fk"] + 256, O["vcm"])
        two("pool", win, O["pool"], "dve")
        two("nq0", win, O["nq"])
        for kv, w in enumerate((A["cmp_w1_k"][0], A["cmp_w1_v"][0])):
            wv_ = w.rearrange("(j p) n -> p j n", p=P)
            for b in range(2):
                piece(f"c{kv}{b}", [(0, wv_[:, 8 * b:8 * b + 8, :])], [("C", 2 * kv + b, 0, 0, None)])
        pair("nq1", win, O["nq"] + 256, O["ksl"])
        piece("fv0", [(0, cols(win, O["fv"], 256))], [("T", t, 0, 256, "act") for t in range(NT)])
        piece("fv1", [(0, cols(win, O["fv"] + 256, P)), (P, cols(win, O["vsl"], P))],
              [("T", t, 0, 256, "act") for t in range(NT)])
        piece("win", [(0, cols(win, O["kwn"], P)), (P, cols(win, O["vwn"], P))],
              [("F", 0, 0, P, "act")] + [("T", t, P, P, "act") for t in range(NT)])
        for b in range(4):
            piece(f"out{b}", [(0, cols(wout, 256 * b, 256))], [("T", t, 0, 256, "dve") for t in range(NT)])
        for b in range(4):
            piece(f"mk{b}", [(0, cols(wk, 256 * b, 256))], [("F", f, f * P, P, "act") for f in range(2)])
        for b in range(4):
            piece(f"mv{b}", [(0, cols(wv, 256 * b, 256))], [("T", t, 0, 256, "act") for t in range(MT)])
        for b in range(4):
            two(f"xq{b}", wq, 256 * b)
        for b in range(4):
            piece(f"xo{b}", [(0, cols(wo, 256 * b, 256))], [("T", t, 0, 256, "dve") for t in range(NT)])
        ND = len(pieces)
        NMP = ND + 4
        ORDER = sorted(KEY, key=KEY.get)
        of_piece = [[g for g, x in enumerate(groups) if x[0] == n] for n in range(ND)]
        raw_need = []
        for n in range(ND):
            before = raw_need[n - RAW] if n >= RAW else 0
            raw_need.append(before + 16 * len(pieces[n]))

        def moe_raw(m):
            i = m % MRAW
            return raw[:, (ND + i) % RAW, :] if i < RAW else raw_x[:, i - RAW, :]

        def moe_full(m):
            i = m % MRAW
            if i < RAW:
                return raw_full[(ND + i) % RAW], raw_need[ND - RAW + i] + 16 * (m // MRAW + 1)
            return rawx_full[i - RAW], 16 * (m // MRAW + 1)

        def moe_split(m):
            i = m % MSPLIT
            if i < SPLIT:
                return whi[:, (ND + i) % SPLIT, :], wlo[:, (ND + i) % SPLIT, :]
            flat = "p k t -> p (k t)"
            return ahi[:, 0:PIECE // T, :].rearrange(flat), alo[:, 0:PIECE // T, :].rearrange(flat)

        LATE_SPLITS = (KEY["win"], ND - 2, ND - 1)

        def evacs(g, eng):
            return sum(x[5] == eng for x in groups[:g + 1])

        UN = []
        for i in range(NT):
            UN += [(i, "c", g, 0) for g in range(NSA_G)] + [(i, "f", h, i + 1) for h in range(FOX_H)]
            UN += [(i, b, h, i + 1) for h in range(NSA_H) for b in "sw"]
        UX = [(i, "x", h, MT) for i in range(NT) for h in range(MEM_H)]

        LAG_T, LAG_V = 3, 5

        class Phase:

            def __init__(self, name, units, col0):
                self.units = units
                self.per = len(units) // NT
                self.col0 = col0
                self.sidx = []
                n = 0
                for x in units:
                    self.sidx.append(n)
                    n += x[1] != "c"
                self.of_s = [u for u, x in enumerate(units) if x[1] != "c"]
                self.scores_done = sem(name + "_scores_done")
                self.max_done = sem(name + "_max_done")
                self.exp_done = sem(name + "_exp_done")
                self.tp_done = sem(name + "_tp_done")
                self.pt_done = sem(name + "_pt_done")
                self.pv_done = sem(name + "_pv_done")
                self.o_done = sem(name + "_o_done")
                self.ot_done = sem(name + "_ot_done")
                self.ot_hi = sem(name + "_ot_hi")
                self.ot_lo = sem(name + "_ot_lo")
                self.blocks = ([list(range(3)), list(range(5, 8))] if name == "A"
                               else [list(range(4)), list(range(4, 8))])
                self.steps = len(units) + LAG_V + 2

            def ot_bank(self, r):
                return ps[4] if r == 2 * NT - 1 else ps[7]

            def score(self, u):
                return 0 <= u < len(self.units) and self.units[u][1] != "c"

            def has(self, u):
                return 0 <= u < len(self.units)

            def rounds(self, k):
                return [(2 * i + b, i, self.blocks[b]) for i in range(NT) for b in range(2)
                        if k == self.per * (i + 1) + LAG_V + (b if i == NT - 1 else 1 + 2 * b)]

        PA = Phase("A", UN, 0)
        PX = Phase("X", UX, 72)

        raw_full = [sem(f"raw_full{i}") for i in range(RAW)]
        rawx_full = [sem(f"rawx_full{i}") for i in range(MRAW - RAW)]
        hi_done = sem("hi_done")
        lo_done = sem("lo_done")
        grp_done = sem("grp_done")
        evac = {"act": sem("evac_act"), "dve": sem("evac_dve")}
        ident_in = sem("ident_in")
        const_in = sem("const_in")
        const2_in = sem("const2_in")
        small_in = sem("small_in")
        rows_in = sem("rows_in")
        x_first = [sem(f"x_first{t}") for t in range(NT)]
        mem_in = [sem(f"mem_in{t}") for t in range(MT)]
        last_in = [sem(f"last_in{t}") for t in range(NT)]
        gain_full = sem("gain_full")
        ss_done = sem("ss_done")
        ms_done = sem("ms_done")
        rms_done = sem("rms_done")
        h_done = sem("h_done")
        ntp_done = sem("ntp_done")
        ntp_hi = sem("ntp_hi")
        ntp_lo = sem("ntp_lo")
        half_set = sem("half_set")
        bf_done = sem("bf_done")
        sm_hi = sem("sm_hi")
        sm_lo = sem("sm_lo")
        smallT_mm = sem("smallT_mm")
        zT_done = sem("zT_done")
        rows_zero = sem("rows_zero")
        small_mm = sem("small_mm")
        z_done = sem("z_done")
        zexp_done = sem("zexp_done")
        lf_done = sem("lf_done")
        gate_done = sem("gate_done")
        cum_mm = sem("cum_mm")
        cum_done = sem("cum_done")
        cumrow_in = sem("cumrow_in")
        kg_done = sem("kg_done")
        f_done = sem("f_done")
        fhi_done = sem("fhi_done")
        flo_done = sem("flo_done")
        steps = sem("pool_steps")
        gelu_done = sem("gelu_done")
        gT_mm = sem("gT_mm")
        gT_done = sem("gT_done")
        kv2_mm = sem("kv2_mm")
        kc_done = sem("kc_done")
        vc_done = sem("vc_done")
        pad_done = sem("pad_done")
        cs_done = sem("cs_done")
        csub_done = sem("csub_done")
        cexp_done = sem("cexp_done")
        pc_done = sem("pc_done")
        pooled_done = sem("pooled_done")
        mix_mm = sem("mix_mm")
        mix_hi = sem("mix_hi")
        mix_lo = sem("mix_lo")
        x_in = [sem(f"x_in{t}") for t in range(NT)]
        dch = sem("dve_chain")
        ach = sem("act_chain")
        route_mm = sem("route_mm")
        rT_done = sem("rT_done")
        logits_done = sem("logits_done")
        r_step = sem("r_step")
        r_exp = sem("r_exp")
        onehot_done = sem("onehot_done")
        rank_mm = sem("rank_mm")
        route_done = sem("route_done")
        hot_done = sem("hot_done")
        list_mm = sem("list_mm")
        list_done = sem("list_done")
        zero_done = sem("zero_done")
        zero_out = sem("zero_out")
        h3_out = [sem(f"h3_out{t}") for t in range(NT)]
        xo_out = sem("xo_out")
        yw_done = sem("yw_done")
        xg_in = sem("xg_in")
        used = sem("moe_piece_used")
        xg_tp = sem("xg_tp")
        xg_hi = sem("xg_hi")
        xg_lo = sem("xg_lo")
        silu_done = sem("silu_done")
        he_done = sem("he_done")
        he_tp = sem("he_tp")
        he_hi = sem("he_hi")
        he_lo = sem("he_lo")
        y_done = sem("y_done")
        y_out = sem("y_out")
        adds_done = sem("adds_done")
        out_done = [sem(f"out_done{t}") for t in range(NT)]

        NX, NM, N2, N3, N4 = 0, NT, NT + MT, 2 * NT + MT, 3 * NT + MT

        block = ctx.enter_context(nc.Block())

        def wait_consumed(eng, n):
            eng.wait_ge(grp_done, of_piece[n][-1] + 1)

        @block.sync
        def _(sp):
            def load_piece(n):
                if n >= RAW:
                    sp.wait_ge(lo_done, n - RAW + 1)
                for c0, src in pieces[n]:
                    w = src.shape[2]
                    dst = raw[:, n % RAW, :].rearrange("p (k n) -> p k n", k=KD)[:, :, c0:c0 + w]
                    sp.dma_start(dst, src).then_inc(raw_full[n % RAW], 16)

            x_t = A["x"][0].rearrange("(t p) d -> t p d", p=P)
            m_t = A["mem"][0].rearrange("(t p) d -> t p d", p=P)
            for t in range(NT):
                sp.dma_start(X[:, t, :], x_t[t]).then_inc(x_first[t], 16)
            load_piece(0)
            sp.dma_start(wsm[:, :, 0:FOX_H], cols(win, O["ff"], FOX_H)).then_inc(small_in, 16)
            sp.dma_start(wsm[:, :, FOX_H:SMALL_W], cols(win, O["gate"], 3 * NSA_H)).then_inc(small_in, 16)
            sp.dma_start(wrt[:, :, 0:NGRP], cols(A["router_coarse_w"][0], 0, NGRP)).then_inc(small_in, 16)
            sp.dma_start(wrt[:, :, NGRP:ROUT_W], cols(A["router_fine_w"][0], 0, NEXP)).then_inc(small_in, 16)
            for n in range(1, KEY["out0"]):
                load_piece(n)
                if n == 4:
                    sp.wait_ge(cum_done, 2)
                    sp.wait_ge(rows_zero, 1)
                    sp.dma_start(Qf[64:65, :, :], cumr[:, 0, :]).then_inc(cumrow_in, 16)
                    sp.dma_start(Kf[65:66, :, :], cumr[:, 1, :]).then_inc(cumrow_in, 16)
            for n in range(KEY["out0"], KEY["out1"] + 1):
                load_piece(n)
            last_fox = max(u for u, x in enumerate(UN) if x[1] == "f")
            sp.wait_ge(PA.scores_done, PA.sidx[last_fox] + 1)
            for t in range(NT):
                sp.dma_start(X[:, t, :], x_t[t]).then_inc(x_in[t], 16)
            load_piece(KEY["out2"])
            sp.wait_ge(PA.pv_done, len(UN))
            for t in range(MT):
                sp.dma_start(tok[:, t, :], m_t[t]).then_inc(mem_in[t], 16)
            for n in range(KEY["out2"] + 1, ND):
                load_piece(n)
            wg, wu, wd = (A[f"exp_w_{c}"][0] for c in ("gate", "up", "down"))

            def load_expert(w, e, half_, m):
                src = w[bass.ds(e, 1), :, :].rearrange("e (k p) f -> p (e k) f", p=P)
                if w is wd:
                    src = src[:, :, 512 * half_:512 * half_ + 512]
                else:
                    src = src[:, KF * half_:KF * half_ + KF, :]
                dst = moe_raw(m).rearrange("p (k f) -> p k f", k=KF)
                sp.dma_start(dst, src).then_inc(moe_full(m)[0], 16)

            for m, (w, e) in enumerate(((wg, 0), (wg, 0), (wu, 0), (wu, 0), (wg, 1), (wg, 1))):
                if m < RAW:
                    sp.wait_ge(lo_done, ND + m - RAW + 1)
                else:
                    sp.wait_ge(grp_done, of_piece[KEY["xo0"]][0] + 1)
                load_expert(w, e, m % 2, m)
            for t in range(NT):
                sp.wait_ge(evac["dve"], evacs(of_piece[ND - 1][t], "dve"))
                sp.dma_start(xod[t * P:(t + 1) * P, :], X[:, t, :]).then_inc(xo_out, 16)
                sp.wait_ge(h_done, N3 + t + 1)
                sp.dma_start(h3d[t * P:(t + 1) * P, :], tok[:, 2 + (N3 + t) % 2, :]).then_inc(h3_out[t], 16)
            sp.wait_ge(route_done, 1)
            turns = sp.value_load(etab[0:1, MAXCH:MAXCH + 1], min_val=NEXP - 2, max_val=MAXCH - 3)
            def load_turn(j, loads):
                for i, (w, e) in enumerate(loads):
                    sp.wait_ge(lo_done, 6 * (j - 1) + (ND + i + 1))
                    load_expert(w, e, i % 2, MRAW + i)

            def expert_of(c):
                return sp.value_load(etab[0:1, bass.ds(c, 1)], min_val=0, max_val=NEXP - 1)

            with sp.Fori(1, turns + 1) as j:
                e, before, after = expert_of(j), expert_of(j - 1), expert_of(j + 1)
                load_turn(j, ((wu, e), (wu, e), (wd, before), (wd, before), (wg, after), (wg, after)))
            e, before = expert_of(turns + 1), expert_of(turns)
            load_turn(turns + 1, ((wu, e), (wu, e), (wd, before), (wd, before), (wd, e), (wd, e)))
            sp.wait_ge(adds_done, 1)
            xo_t = xod[0:T, :].rearrange("(t p) d -> t p d", p=P)
            out_t = out[0].rearrange("(t p) d -> t p d", p=P)
            for t in range(NT):
                sp.dma_start(X[:, t, :], xo_t[t]).then_inc(last_in[t], 16)
            for t in range(NT):
                sp.wait_ge(h_done, N4 + t + 1)
                sp.dma_start(out_t[t], tok[:, t, :]).then_inc(out_done[t], 16)
            for t in range(NT):
                sp.wait_ge(out_done[t], 16)

        @block.gpsimd
        def _(pool):
            pool.memset(half[:, :], -0.5).then_inc(half_set, 1)
            pool.memset(spare[:, 0:1], 0.0).then_inc(half_set, 1)
            pool.memset(zeroi[:, :], 0).then_inc(half_set, 1)
            pool.wait_ge(half_set, 3)

            def rms(q):
                pool.wait_ge(ms_done, q + 1)
                pool.tensor_tensor(stat[:, 2, q:q + 1], stat[:, 1, q:q + 1], half[:, :], ALU.pow).then_inc(rms_done, 1)

            for q in range(NT):
                rms(q)
            pool.dma_start(tri, C["tri"]).then_inc(const_in, 16)
            pool.dma_start(bias24[:, 0:FOX_H], A["fox_forget_b"].to_broadcast([P, FOX_H])).then_inc(const_in, 16)
            pool.dma_start(bias24[:, FOX_H:], A["nsa_gate_b"].to_broadcast([P, 3 * NSA_H])).then_inc(const_in, 16)
            for kv, c in enumerate("kv"):
                pool.dma_start(pe2[:, kv, :], A[f"pe_{c}"]).then_inc(const_in, 16)
            pool.dma_start(bf_stage, C["bf"]).then_inc(const2_in, 16)
            pool.dma_start(pcon[:, :, :], C["pool"]).then_inc(const2_in, 16)
            pool.dma_start(pscale_t[:, :], A["pscale"]).then_inc(const2_in, 16)
            for kv, c in enumerate("kv"):
                pool.dma_start(w2[:, kv, :, :], A[f"cmp_w2_{c}"][0].rearrange("(k p) n -> p k n", p=P))\
                    .then_inc(const2_in, 16)
            pool.wait_ge(pad_done, 1)
            for g in range(4):
                lo = DH * (g % 2)
                pool.dma_start(wpool[lo:lo + DH, g // 2, lo:lo + DH], A["pool_w"][0, g]).then_inc(const2_in, 16)
            pool.dma_start(tabs[:, :], C["tabs"]).then_inc(const2_in, 16)
            pool.dma_start(rbias[:, 0:NGRP], A["router_coarse_b"].to_broadcast([P, NGRP])).then_inc(const2_in, 16)
            pool.dma_start(rbias[:, NGRP:], A["router_fine_b"].to_broadcast([P, NEXP])).then_inc(const2_in, 16)
            pool.wait_ge(h_done, NT)
            pool.memset(arena[64:P, 0:qk_end], 0.0).then_inc(rows_zero, 1)
            pool.wait_ge(rows_zero, 1)
            pool.dma_start(Qn[64:66, :, :], C["qrows"]).then_inc(rows_in, 16)
            pool.dma_start(Ks[64:66, :, :], C["krows"]).then_inc(rows_in, 16)
            pool.dma_start(Kw[64:66, :, :], C["krows"]).then_inc(rows_in, 16)
            pool.dma_start(Kc[64:66, :, :], C["crows"]).then_inc(rows_in, 16)
            pool.dma_start(Qf[65:66, :, :], C["ones"]).then_inc(rows_in, 16)
            pool.dma_start(Kf[64:65, :, :], C["ones"]).then_inc(rows_in, 16)
            for q in range(NT, N4):
                rms(q)
            pool.wait_ge(list_done, 2)
            pool.wait_ge(route_done, 1)
            turns = pool.value_load(etab[0:1, MAXCH:MAXCH + 1], min_val=NEXP - 2, max_val=MAXCH - 3)
            pool.wait_ge(zero_out, 32)
            for t in range(NT):
                pool.wait_ge(h3_out[t], 16)
            pool.wait_ge(xo_out, 16 * NT)

            def copy_tokens(dst, c):
                pool.tensor_tensor(dst[0:CHUNK, :], ltok[0:CHUNK, bass.ds(c, 1)], zeroi[0:CHUNK, :], ALU.add).then_inc(steps, 1)

            def copy_weights(c):
                pool.tensor_tensor(yw[0:CHUNK, :], lwt[0:CHUNK, bass.ds(c, 1)], spare[0:CHUNK, 0:1], ALU.add)\
                    .then_inc(yw_done, 1)

            def pause():
                pool.tensor_tensor(spare[:, 1:2], spare[:, 0:1], spare[:, 0:1], ALU.add).then_inc(steps, 1)

            def gather():
                pool.indirect_dma_start(tok[0:CHUNK, 0, :], None, h3d,
                                        bass.IndirectOffsetOnAxis(ap=xidx[0:CHUNK, :], axis=0)).then_inc(xg_in, 16)

            def add():
                pool.indirect_dma_start(xod, bass.IndirectOffsetOnAxis(ap=yidx[0:CHUNK, :], axis=0),
                                        tok[0:CHUNK, 2, :], None, compute_op=ALU.add).then_inc(y_out, 16)

            for c in range(3):
                if c:
                    pool.wait_ge(xg_in, 16 * c)
                    pool.wait_ge(xg_tp, 2 * c)
                copy_tokens(xidx, c)
                pool.wait_ge(steps, c + 1)
                gather()
            copy_weights(0)
            with pool.Fori(1, turns + 2) as j:
                pool.wait_ge(xg_in, 16 * j + 32)
                pool.wait_ge(xg_tp, 2 * j + 4)
                copy_tokens(xidx, j + 2)
                pool.wait_ge(steps, 4 * j)
                pause()
                gather()
                copy_tokens(yidx, j - 1)
                pool.wait_ge(steps, 4 * j + 2)
                pool.wait_ge(y_done, 2 * j)
                pause()
                add()
                pool.wait_ge(y_out, 16 * j)
                copy_weights(j)
            copy_tokens(yidx, turns + 1)
            pool.wait_ge(steps, 4 * turns + 8)
            pool.wait_ge(y_done, 2 * turns + 4)
            pause()
            add()
            pool.wait_ge(y_out, 16 * turns + 32)
            pool.wait_ge(xg_in, 16 * turns + 64)
            pool.wait_ge(steps, 4 * turns + 9)
            pool.tensor_tensor(spare[:, 1:2], spare[:, 0:1], spare[:, 0:1], ALU.add).then_inc(adds_done, 1)
            for q in range(N4, N4 + NT):
                rms(q)

        @block.scalar
        def _(act):
            a = nc.scalar
            chain = [0]

            def link(ins):
                chain[0] += 1
                ins.then_inc(ach, 1)
                act.wait_ge(ach, chain[0])

            act.dma_start(ident[:, :], C["ident"]).then_inc(ident_in, 16)
            g_mix, g_x, g_m, g_f, g_o = (A[n] for n in ("mix_norm_g", "xattn_norm_g", "mem_norm_g", "ffn_norm_g",
                                                        "final_norm_g"))
            act.dma_start(gbc[:, :], g_mix.to_broadcast([P, D])).then_inc(gain_full, 16)

            def split(n):
                act.wait_ge(raw_full[n % RAW], raw_need[n])
                if n >= SPLIT:
                    wait_consumed(act, n - SPLIT)
                a.activation(whi[:, n % SPLIT, :], raw[:, n % RAW, :], ACT.Copy).then_inc(hi_done, 1)

            def split_expert(m, j=None):
                full, need = moe_full(m)
                act.wait_ge(full, need if j is None else 16 * (j - 1) + need)
                if m < SPLIT:
                    wait_consumed(act, ND + m - SPLIT)
                elif m < MSPLIT:
                    act.wait_ge(route_mm, 1)
                else:
                    free = m - MSPLIT + 1
                    act.wait_ge(used, free if j is None else 6 * (j - 1) + free)
                a.activation(moe_split(m)[0], moe_raw(m), ACT.Copy).then_inc(hi_done, 1)

            def square(q, src, dst=None):
                if q >= 2 and q < N4:
                    act.wait_ge(ntp_done, 2 * (q - 1))
                a.activation(tok[:, 2 + q % 2, :] if dst is None else dst, src, ACT.Square, accum_out=stat[:, 0, q:q + 1]).then_inc(ss_done, 1)

            def norm_hi(q, dst, t):
                for b in range(2):
                    act.wait_ge(ntp_done, 2 * q + b + 1)
                    src = ps[4 + 2 * (q % 2) + b][:, :].rearrange("p (k t) -> p k t", k=4)
                    a.activation(dst[:, 4 * b:4 * b + 4, t * P:(t + 1) * P], src, ACT.Copy).then_inc(ntp_hi, 1)

            def heads_out(dst, h0, bank, scale, last_inc=True):
                a.activation(dst[0:64, h0, :], bank[0:64, :], ACT.Copy, scale=scale)
                return a.activation(dst[0:64, h0 + 1, :], bank[64:128, :], ACT.Copy, scale=scale)

            def compress_in(kv, bank):
                for g in range(NSA_G):
                    a.activation(KG[kv][0:64, g, :], bank[64 * g:64 * g + 64, :], ACT.Copy)
                    ins = a.activation(KG[kv][64:128, g, 0:T - 1], bank[64 * g:64 * g + 64, 1:T], ACT.Copy)
                return ins

            def evacuate(n):
                key = ORDER[n]
                for g in of_piece[n]:
                    _, kind, idx, c0, w, eng = groups[g]
                    if eng != "act":
                        continue
                    act.wait_ge(grp_done, g + 1)
                    b = ps[g % DRING]
                    if key == "fq0":
                        ins = heads_out(Qf, 2 * idx, b, DH ** -0.5)
                    elif key == "fk0":
                        ins = heads_out(Kf, 2 * idx, b, 1.0)
                    elif key in ("fq1", "fk1"):
                        kv = key == "fk1"
                        if idx == 0:
                            ins = heads_out(Kf if kv else Qf, 4, b, 1.0 if kv else DH ** -0.5)
                        else:
                            ins = compress_in(int(kv), b)
                    elif key == "nq0":
                        ins = heads_out(Qn, 2 * idx, b, DH ** -0.5)
                    elif key == "nq1":
                        ins = heads_out(Qn, 4, b, DH ** -0.5) if idx == 0 else heads_out(Ks, 0, b, 1.0)
                    elif key == "fv0":
                        ins = a.activation(Vf[:, idx, 0:256], b[:, 0:256], ACT.Copy)
                    elif key == "fv1":
                        a.activation(Vf[:, idx, 256:384], b[:, 0:P], ACT.Copy)
                        ins = a.activation(Vs[:, idx, :], b[:, P:2 * P], ACT.Copy)
                    elif key == "win":
                        ins = heads_out(Kw, 0, b, 1.0) if kind == "F" else \
                            a.activation(Vw[:, idx, :], b[:, 0:P], ACT.Copy)
                    elif key[:2] == "mk":
                        ins = a.activation(KTm[:, 2 * int(key[2]) + idx, :], b[:, 0:MEM], ACT.Copy)
                    elif key[:2] == "mv":
                        c = 256 * int(key[2])
                        ins = a.activation(Vm[:, idx, c:c + 256], b[:, 0:256], ACT.Copy)
                    else:
                        assert key[:2] == "xq"
                        ins = a.activation(QTx[:, 2 * int(key[2]) + idx, :], b[:, :], ACT.Copy,
                                           scale=(D // MEM_H) ** -0.5)
                    ins.then_inc(evac["act"], 1)

            def split_after(n):
                if n + SPLIT < ND:
                    split(n + SPLIT)
                else:
                    split_expert(n + SPLIT - ND)

            def dense(n):
                evacuate(n)
                if n not in LATE_SPLITS:
                    split_after(n)

            for t in range(NT):
                act.wait_ge(x_first[t], 16)
                square(NX + t, X[:, t, :])
                if t >= 1:
                    norm_hi(NX + t - 1, ahi, t - 1)
                if t == 2:
                    split(0)
            norm_hi(NX + NT - 1, ahi, NT - 1)
            split(1)
            act.wait_ge(small_in, 16 * 4)
            a.activation(wsm_hi[:, :, :], wsm[:, :, :], ACT.Copy).then_inc(sm_hi, 1)
            a.activation(wrt_hi[:, :, :], wrt[:, :, :], ACT.Copy).then_inc(sm_hi, 1)
            dense(0)
            dense(1)
            act.wait_ge(z_done, 1)
            a.activation(zz[:, 2, :, :], zz[:, 1, :, :], ACT.Exp).then_inc(zexp_done, 1)
            act.wait_ge(zexp_done, 1)
            a.activation(zz[:, 3, :, 0:FOX_H], zz[:, 2, :, 0:FOX_H], ACT.Ln, bias=1.0).then_inc(zexp_done, 1)
            act.wait_ge(f_done, 1)
            a.activation(fhi[0].rearrange("p j m -> p (j m)"), Fb.rearrange("p a b c -> p (a b c)"),
                         ACT.Copy).then_inc(fhi_done, 1)
            dense(2)
            act.wait_ge(cum_mm, 1)
            a.activation(cumr[:, 0, :], ps[5][0:FOX_H, :], ACT.Copy).then_inc(cum_done, 1)
            a.activation(cumr[:, 1, :], ps[5][0:FOX_H, :], ACT.Copy, scale=-1.0).then_inc(cum_done, 1)
            dense(3)
            act.wait_ge(f_done, 2)
            a.activation(fhi[1].rearrange("p j m -> p (j m)"), Fb.rearrange("p a b c -> p (a b c)"),
                         ACT.Copy).then_inc(fhi_done, 1)
            for n in range(4, KEY["out0"]):
                dense(n)
                key = ORDER[n]
                if key in ("c01", "c11"):
                    kv = int(key[1])
                    act.wait_ge(grp_done, of_piece[n][-1] + 1)
                    act.wait_ge(pooled_done, 2)
                    a.activation(gtok[:, kv, :], ps[6 + kv][0:2 * N_CMP, 0:CMP_HID], ACT.Gelu_apprx_tanh)\
                        .then_inc(gelu_done, 1)
                if key == "nq1":
                    act.wait_ge(gT_mm, 1)
                    a.activation(gT[:, :, :, :].rearrange("p a b c -> p (a b c)"), ps[6][:, 0:8 * N_CMP], ACT.Copy)\
                        .then_inc(gT_done, 1)
                if key == "fv0":
                    act.wait_ge(kv2_mm, 2)
                    act.wait_ge(pad_done, 1)
                    a.activation(Kc[0:64, :, 0:N_CMP], ps[4][0:64, 0:2 * N_CMP].rearrange("p (g c) -> p g c", g=NSA_G),
                                 ACT.Copy).then_inc(kc_done, 1)
                if key == "fv1":
                    for b in range(2):
                        act.wait_ge(csub_done, b + 1)
                        v = Pc[:, :, NSA_R * b:NSA_R * (b + 1), :]
                        a.activation(v, v, ACT.Exp).then_inc(cexp_done, 1)
            act.wait_ge(const2_in, 16 * N_CONST2)
            for f in range(2):
                act.wait_ge(mix_mm, f + 1)
                a.activation(ahi[:, 3 + f, :], ps[6 + f][:, :], ACT.Copy, scale=pscale[:, f, :]).then_inc(mix_hi, 1)
            split_after(KEY["win"])

            def attention(ph):
                for k in range(ph.steps):
                    if ph.score(k):
                        s = ph.sidx[k]
                        nk = P * ph.units[k][3]
                        act.wait_ge(ph.max_done, s + 1)
                        if s >= len(Pr):
                            act.wait_ge(ph.tp_done, ph.of_s[s - len(Pr)] + 1)
                        c = ph.col0 + s
                        a.activation(Pr[s % len(Pr)][:, 0:nk], ps[s % 3][:, 0:nk], ACT.Exp, bias=nmax[:, c:c + 1],
                                     accum_out=den[:, c:c + 1]).then_inc(ph.exp_done, 1)
                    u = k - LAG_T
                    if ph.has(u):
                        i, kind, h, nb = ph.units[u]
                        act.wait_ge(ph.tp_done, u + 1)
                        if u >= len(PTr):
                            act.wait_ge(ph.pv_done, u - len(PTr) + 1)
                        rows_, w = (NSA_R * CMP_PAD, P) if kind == "c" else (P, P * nb)
                        a.activation(PTr[u % len(PTr)][0:rows_, 0:w], ps[3 + u % 2][0:rows_, 0:w], ACT.Copy)\
                            .then_inc(ph.pt_done, 1)
                    for r, i, fb in ph.rounds(k):
                        act.wait_ge(ph.ot_done, r + 1)
                        src = ph.ot_bank(r)[:, 0:P * len(fb)].rearrange("p (k t) -> p k t", k=len(fb))
                        a.activation(ahi[:, fb[0]:fb[0] + len(fb), i * P:(i + 1) * P], src, ACT.Copy)\
                            .then_inc(ph.ot_hi, 1)

            attention(PA)
            act.wait_ge(h_done, NM)
            act.dma_start(gbc[:, :], g_m.to_broadcast([P, D])).then_inc(gain_full, 16)
            dense(KEY["out0"])
            for t in range(MT):
                q = NM + t
                act.wait_ge(mem_in[t], 16)
                act.wait_ge(PA.ot_done, 2 * NT)
                square(q, tok[:, t, :])
            dense(KEY["out1"])
            for t in range(MT):
                norm_hi(NM + t, memhi, t)
            act.wait_ge(h_done, NM + MT)
            act.dma_start(gbc[:, :], g_x.to_broadcast([P, D])).then_inc(gain_full, 16)
            dense(KEY["out2"])
            dense(KEY["out3"])
            for t in range(NT):
                act.wait_ge(evac["dve"], evacs(of_piece[KEY["out3"]][t], "dve"))
                square(N2 + t, X[:, t, :])
                dense(KEY["mk0"] + t)
                if t:
                    norm_hi(N2 + t - 1, ahi, t - 1)
            norm_hi(N2 + NT - 1, ahi, NT - 1)
            act.wait_ge(h_done, N3)
            act.dma_start(gbc[:, :], g_f.to_broadcast([P, D])).then_inc(gain_full, 16)
            for n in range(KEY["mv0"], KEY["xo0"]):
                dense(n)
            attention(PX)
            for n in range(KEY["xo0"], ND):
                dense(n)
            act.wait_ge(zero_done, 1)
            act.dma_start(h3d[T:T + P, :], tok[:, 0, :]).then_inc(zero_out, 16)
            act.dma_start(xod[T:T + P, :], tok[:, 0, :]).then_inc(zero_out, 16)
            for t in range(NT):
                act.wait_ge(evac["dve"], evacs(of_piece[ND - 1][t], "dve"))
                if t >= 2:
                    act.wait_ge(h3_out[t - 2], 16)
                square(N3 + t, X[:, t, :])
                if t:
                    norm_hi(N3 + t - 1, ahi, t - 1)
            norm_hi(N3 + NT - 1, ahi, NT - 1)
            split_after(ND - 2)
            split_after(ND - 1)
            act.dma_start(gbc[:, :], g_o.rearrange("(a n) -> a n", a=1).to_broadcast([P, D])).then_inc(gain_full, 16)
            R = work[:, 0:2048]
            act.wait_ge(r_step, 1)
            a.activation(R[:, 96:112], R[:, 80:96], ACT.Exp).then_inc(r_exp, 1)
            act.wait_ge(r_step, 2)
            a.activation(R[:, 392:396], R[:, 388:392], ACT.Exp).then_inc(r_exp, 1)

            def xg_hi_out(n):
                for b in range(2):
                    act.wait_ge(xg_tp, n + b + 1)
                    a.activation(xghi[:, 4 * b:4 * b + 4, :], ps[2 + b][:, 0:4 * CHUNK].rearrange("p (k t) -> p k t", k=4),
                                 ACT.Copy).then_inc(xg_hi, 1)

            def silu(n_used, j):
                act.wait_ge(used, n_used)
                act.wait_ge(he_done, j)
                a.activation(sg, ps[0][0:CHUNK, :], ACT.Silu).then_inc(silu_done, 1)

            def he_hi_out(n):
                act.wait_ge(he_tp, n)
                a.activation(hehi, ps[6][:, 0:KF * CHUNK].rearrange("p (k t) -> p k t", k=KF), ACT.Copy).then_inc(he_hi, 1)

            def y_out_half(b, n_used):
                act.wait_ge(used, n_used)
                a.activation(tok[0:CHUNK, 2, 512 * b:512 * b + 512], ps[4 + b][0:CHUNK, :], ACT.Copy,
                             scale=yw[0:CHUNK, :]).then_inc(y_done, 1)

            split_expert(2)
            xg_hi_out(0)
            split_expert(3)
            split_expert(4)
            silu(2, 1)
            split_expert(5)
            split_expert(6)
            xg_hi_out(2)
            he_hi_out(1)
            act.wait_ge(route_done, 1)
            turns = act.value_load(etab[0:1, MAXCH:MAXCH + 1], min_val=NEXP - 2, max_val=MAXCH - 3)

            def turn(j, last):
                base = 6 * (j - 1) + 4
                split_expert(7, j)
                split_expert(8, j)
                silu(base + 2, j + 1)
                split_expert(9, j)
                split_expert(10, j)
                xg_hi_out(2 * j + 2)
                split_expert(11, j)
                act.wait_ge(yw_done, j)
                y_out_half(0, base + 5)
                if not last:
                    split_expert(12, j)
                y_out_half(1, base + 6)
                he_hi_out(j + 1)

            with act.Fori(1, turns + 1) as j:
                turn(j, False)
            turn(turns + 1, True)
            act.wait_ge(yw_done, turns + 2)
            y_out_half(0, 6 * turns + 11)
            y_out_half(1, 6 * turns + 12)
            for t in range(NT):
                q = N4 + t
                act.wait_ge(last_in[t], 16)
                square(q, X[:, t, :], tok[:, t, :])

        @block.vector
        def _(dve):
            v = nc.vector
            chain = [0]

            def mark(ins):
                chain[0] += 1
                ins.then_inc(dch, 1)
                return chain[0]

            def link(ins):
                dve.wait_ge(dch, mark(ins))

            link(v.memset(wpool[:, :, :], 0.0))
            link(v.memset(Vc[0:NSA_R * CMP_PAD, :, :], 0.0))
            v.memset(Kc[:, :, :], 0.0).then_inc(pad_done, 1)

            def split(n):
                dve.wait_ge(hi_done, n + 1)
                v.tensor_tensor(wlo[:, n % SPLIT, :], raw[:, n % RAW, :], whi[:, n % SPLIT, :].bitcast(F32),
                                ALU.subtract).then_inc(lo_done, 1)

            def split_expert(m, j=None):
                n = ND + m + 1
                dve.wait_ge(hi_done, n if j is None else 6 * (j - 1) + n)
                hi, lo = moe_split(m)
                v.tensor_tensor(lo, moe_raw(m), hi.bitcast(F32), ALU.subtract).then_inc(lo_done, 1)

            def norm(q, src, dst=None):
                dve.wait_ge(ss_done, q + 1)
                v.tensor_scalar(stat[:, 1, q:q + 1], stat[:, 0, q:q + 1], 1.0 / D, EPS, ALU.mult, ALU.add)\
                    .then_inc(ms_done, 1)
                dve.wait_ge(rms_done, q + 1)
                v.scalar_tensor_tensor(tok[:, 2 + q % 2, :] if dst is None else dst, src, stat[:, 2, q:q + 1], gbc[:, :],
                                       ALU.mult, ALU.mult).then_inc(h_done, 1)

            def norm_lo(q, dst, hi, t):
                for b in range(2):
                    dve.wait_ge(ntp_hi, 2 * q + b + 1)
                    src = ps[4 + 2 * (q % 2) + b][:, :].rearrange("p (k t) -> p k t", k=4)
                    sl = (slice(None), slice(4 * b, 4 * b + 4), slice(t * P, (t + 1) * P))
                    v.tensor_tensor(dst[sl], src, hi[sl].bitcast(F32), ALU.subtract).then_inc(ntp_lo, 1)

            def pool_tile(f, bank):
                v.tensor_copy(Ub[:, 16:UW], bank[:, :]).then_inc(evac["dve"], 1)
                dve.wait_ge(evac["dve"], f + 1)
                lo_w = POOL_WINDOWS[2 * f]
                src, dst = Ub, Sa
                width = 1
                spans = {}
                while width < POOL_WINDOWS[2 * f + 1]:
                    s = 2 * width - 1
                    link(v.tensor_tensor(dst[:, s:UW], src[:, s:UW], src[:, s - width:UW - width], ALU.add))
                    width *= 2
                    if width == lo_w:
                        emit_rows(f, 0, dst)
                    src, dst = dst, (Sb if dst is Sa else Sa)
                emit_rows(f, 1, src)

            def emit_rows(f, half_, s):
                r = slice(64 * half_, 64 * half_ + 64)
                link(v.tensor_tensor(pooled[r, f, 0:16], s[r, 16:32], corr[r, f, :], ALU.mult))
                link(v.scalar_tensor_tensor(pooled[r, f, 0:16], pooled[r, f, 0:16], invw[r, f, :],
                                            Ub[r, 16:32], ALU.mult, ALU.subtract))
                ins = v.scalar_tensor_tensor(pooled[r, f, 16:T], s[r, 32:UW], invw[r, f, :], Ub[r, 32:UW],
                                             ALU.mult, ALU.subtract)
                if half_:
                    ins.then_inc(pooled_done, 1)
                    dve.wait_ge(pooled_done, f + 1)

            def compress_blocks(kv):
                g_kcm = of_piece[KEY["fq1" if kv == 0 else "fk1"]][1]
                dve.wait_ge(evac["act"], evacs(g_kcm, "act"))
                if kv:
                    dve.wait_ge(fhi_done, 1)
                    dve.wait_ge(flo_done, 1)
                for g in range(NSA_G):
                    src = KG[kv][:, g, :]
                    a0 = src[:, 0:N_CMP * 16].rearrange("p (c j e) -> p j c e", j=8, e=2)[:, :, :, 0]
                    a1 = src[:, 16:16 + N_CMP * 16].rearrange("p (c j e) -> p j c e", j=8, e=2)[:, :, :, 0]
                    for b, s in enumerate((a0, a1)):
                        pe_b = pe2[:, kv, 8 * b:8 * b + 8].unsqueeze(2).to_broadcast([P, 8, N_CMP])
                        ins = v.tensor_tensor(Fb[:, 8 * b:8 * b + 8, g, :], s, pe_b, ALU.add)
                        if (g, b) == (1, 1):
                            ins.then_inc(f_done, 1)
                dve.wait_ge(fhi_done, kv + 1)
                v.tensor_tensor(flo[kv].rearrange("p j m -> p (j m)"), Fb.rearrange("p a b c -> p (a b c)"),
                                fhi[kv].rearrange("p j m -> p (j m)").bitcast(F32), ALU.subtract).then_inc(flo_done, 1)

            def evacuate(n, only=range(NT)):
                key = ORDER[n]
                for g in of_piece[n]:
                    _, kind, idx, c0, w, eng = groups[g]
                    if idx not in only:
                        continue
                    if eng != "dve":
                        continue
                    dve.wait_ge(grp_done, g + 1)
                    b = ps[g % DRING]
                    if key == "pool":
                        pool_tile(idx, b)
                    else:
                        c = 256 * int(key[-1])
                        if key == "out0":
                            dve.wait_ge(x_in[idx], 16)
                        v.tensor_tensor(X[:, idx, c:c + 256], b[:, 0:256], X[:, idx, c:c + 256], ALU.add)\
                            .then_inc(evac["dve"], 1)

            def split_after(n):
                if n + SPLIT < ND:
                    split(n + SPLIT)
                else:
                    split_expert(n + SPLIT - ND)

            def dense(n):
                evacuate(n)
                if n not in LATE_SPLITS:
                    split_after(n)

            dve.wait_ge(half_set, 3)
            dve.wait_ge(gain_full, 16)
            for t in range(NT):
                norm(NX + t, X[:, t, :])
                if t >= 1:
                    norm_lo(NX + t - 1, alo, ahi, t - 1)
                if t == 2:
                    split(0)
            norm_lo(NX + NT - 1, alo, ahi, NT - 1)
            split(1)
            dve.wait_ge(sm_hi, 2)
            v.tensor_tensor(wsm_lo[:, :, :], wsm[:, :, :], wsm_hi[:, :, :].bitcast(F32), ALU.subtract).then_inc(sm_lo, 1)
            v.tensor_tensor(wrt_lo[:, :, :], wrt[:, :, :], wrt_hi[:, :, :].bitcast(F32), ALU.subtract).then_inc(sm_lo, 1)
            dense(0)
            dve.wait_ge(smallT_mm, 1)
            v.tensor_copy(zT, ps[5][0:SMALL_W, :]).then_inc(zT_done, 1)
            dense(1)
            dve.wait_ge(const_in, 16 * N_CONST)
            dve.wait_ge(small_mm, 1)
            z4 = ps[4][:, 0:NT * SMALL_W].rearrange("p (t c) -> p t c", t=NT)
            bb = bias24[:, :].unsqueeze(1).to_broadcast([P, NT, SMALL_W])
            link(v.tensor_tensor(zz[:, 0, :, :], z4, bb, ALU.add))
            link(v.tensor_scalar(zz[:, 1, :, :], zz[:, 0, :, :], -1.0, None, ALU.mult))
            link(v.tensor_tensor(zz[:, 1, :, 0:FOX_H], zz[:, 0, :, 0:FOX_H], zz[:, 1, :, 0:FOX_H], ALU.min))
            v.tensor_scalar(zz[:, 4, :, 0:FOX_H], zz[:, 0, :, 0:FOX_H], 0.0, None, ALU.min).then_inc(z_done, 1)
            dve.wait_ge(zexp_done, 2)
            dve.wait_ge(z_done, 1)
            v.tensor_tensor(zz[:, 4, :, 0:FOX_H], zz[:, 4, :, 0:FOX_H], zz[:, 3, :, 0:FOX_H], ALU.subtract)\
                .then_inc(lf_done, 1)
            link(v.tensor_scalar(zz[:, 5, :, FOX_H:], zz[:, 2, :, FOX_H:], 1.0, None, ALU.add))
            v.reciprocal(zz[:, 5, :, FOX_H:], zz[:, 5, :, FOX_H:]).then_inc(gate_done, 1)
            compress_blocks(0)
            dense(2)
            dense(3)
            compress_blocks(1)
            dve.wait_ge(const2_in, 16 * N_CONST2)
            v.tensor_copy(bfc[:, :], bf_stage).then_inc(bf_done, 1)
            dve.wait_ge(bf_done, 1)
            dve.wait_ge(cum_mm, 1)
            dve.wait_ge(cumrow_in, 32)
            link(v.memset(Ub[:, 0:16], 0.0))
            link(v.memset(Sa[:, 0:16], 0.0))
            link(v.memset(Sb[:, 0:16], 0.0))
            for n in range(4, KEY["out0"]):
                dense(n)
                if ORDER[n] == "fv0":
                    dve.wait_ge(kv2_mm, 2)
                    for g in range(NSA_G):
                        for r in range(NSA_R):
                            ins = v.tensor_copy(Vc[CMP_PAD * r:CMP_PAD * r + N_CMP, g, DH * r:DH * (r + 1)],
                                                ps[5][0:N_CMP, DH * g:DH * (g + 1)])
                    ins.then_inc(vc_done, 1)
                if ORDER[n] == "fv1":
                    HB = NSA_R * NT
                    for b in range(2):
                        dve.wait_ge(cs_done, b + 1)
                        s3 = ps[6 + b][:, 0:HB * CMP_PAD].rearrange("p (i r c) -> p i r c", i=NT, c=CMP_PAD)
                        p3 = Pc[:, :, NSA_R * b:NSA_R * (b + 1), :]
                        m = cst[:, 0, HB * b:HB * (b + 1)].rearrange("p (i r) -> p i r", i=NT)
                        link(v.tensor_reduce(m, s3, AX.X, ALU.max))
                        link(v.tensor_scalar(m, m, -1e20, None, ALU.max))
                        v.tensor_tensor(p3, s3, m.unsqueeze(3).to_broadcast([P, NT, NSA_R, CMP_PAD]), ALU.subtract)\
                            .then_inc(csub_done, 1)
                    dve.wait_ge(cexp_done, 2)
                    pall = Pc.rearrange("p a b c -> p (a b) c")
                    link(v.tensor_reduce(cst[:, 1, :], pall, AX.X, ALU.add))
                    link(v.tensor_scalar(cst[:, 2, :], cst[:, 1, :], 1e-30, None, ALU.max))
                    link(v.reciprocal(cst[:, 3, :], cst[:, 2, :]))
                    dve.wait_ge(gate_done, 1)
                    gates = zz[:, 5, :, FOX_H:].rearrange("p t (h b) -> p t h b", b=3)
                    link(v.tensor_tensor(cst[:, 4, :].rearrange("p (t h) -> p t h", t=NT),
                                         cst[:, 3, :].rearrange("p (t h) -> p t h", t=NT), gates[:, :, :, 0], ALU.mult))
                    v.tensor_tensor(pall, pall, cst[:, 4, :].unsqueeze(2).to_broadcast([P, 2 * HB, CMP_PAD]), ALU.mult)\
                        .then_inc(pc_done, 1)
            for f in range(2):
                dve.wait_ge(mix_hi, f + 1)
                v.scalar_tensor_tensor(alo[:, 3 + f, :], ps[6 + f][:, :], pscale[:, f, :],
                                       ahi[:, 3 + f, :].bitcast(F32), ALU.mult, ALU.subtract).then_inc(mix_lo, 1)
            split_after(KEY["win"])

            def attention(ph):
                marks = {}
                for k in range(ph.steps):
                    if ph.score(k):
                        s = ph.sidx[k]
                        nk = P * ph.units[k][3]
                        dve.wait_ge(ph.scores_done, s + 1)
                        c = ph.col0 + s
                        v.tensor_reduce(nmax[:, c:c + 1], ps[s % 3][:, 0:nk], AX.X, ALU.max, negate=True)\
                            .then_inc(ph.max_done, 1)
                    u = k - 1
                    if ph.score(u):
                        s = ph.sidx[u]
                        c = ph.col0 + s
                        dve.wait_ge(ph.exp_done, s + 1)
                        marks[u] = mark(v.reciprocal(rden[:, c:c + 1], den[:, c:c + 1]))
                    u = k - LAG_V
                    if ph.has(u):
                        i, kind, h, nb = ph.units[u]
                        c = ph.col0 + ph.sidx[u]
                        dve.wait_ge(ph.pv_done, u + 1)
                        ot = tok[:, 2 + i % 2, :]
                        if u % ph.per == 0 and i >= 2:
                            dve.wait_ge(ph.ot_done, 2 * (i - 1))
                        b = ps[5 + u % 2]
                        if kind == "c":
                            w = NSA_R * DH
                            c0 = FOX_W + POOL_W + h * w
                            v.tensor_copy(ot[:, c0:c0 + w], b[:, 0:w]).then_inc(ph.o_done, 1)
                        elif kind in "fx":
                            w = DH if kind == "f" else D // MEM_H
                            dve.wait_ge(dch, marks[u])
                            v.tensor_scalar(ot[:, h * w:h * w + w], b[:, 0:w], rden[:, c:c + 1], None, ALU.mult)\
                                .then_inc(ph.o_done, 1)
                        else:
                            c0 = FOX_W + POOL_W + h * DH
                            dve.wait_ge(dch, marks[("g", u)])
                            dve.wait_ge(ph.o_done, u)
                            v.scalar_tensor_tensor(ot[:, c0:c0 + DH], b[:, 0:DH], coef[:, c:c + 1], ot[:, c0:c0 + DH],
                                                   ALU.mult, ALU.add).then_inc(ph.o_done, 1)
                    u = k - 1
                    if ph.score(u) and ph.units[u][1] in "sw":
                        i, kind, h, nb = ph.units[u]
                        c = ph.col0 + ph.sidx[u]
                        gate = zz[:, 5, i, FOX_H + 3 * h + 1 + (kind == "w"):FOX_H + 3 * h + 2 + (kind == "w")]
                        dve.wait_ge(dch, marks[u])
                        marks[("g", u)] = mark(v.tensor_tensor(coef[:, c:c + 1], rden[:, c:c + 1], gate, ALU.mult))
                    for r, i, fb in ph.rounds(k):
                        dve.wait_ge(ph.ot_hi, r + 1)
                        src = ph.ot_bank(r)[:, 0:P * len(fb)].rearrange("p (k t) -> p k t", k=len(fb))
                        sl = (slice(None), slice(fb[0], fb[0] + len(fb)), slice(i * P, (i + 1) * P))
                        v.tensor_tensor(alo[sl], src, ahi[sl].bitcast(F32), ALU.subtract).then_inc(ph.ot_lo, 1)

            attention(PA)
            dense(KEY["out0"])
            dve.wait_ge(gain_full, 32)
            for t in range(MT):
                norm(NM + t, tok[:, t, :])
            dense(KEY["out1"])
            for t in range(MT):
                norm_lo(NM + t, memlo, memhi, t)
            dense(KEY["out2"])
            dense(KEY["out3"])
            dve.wait_ge(gain_full, 48)
            for t in range(NT):
                norm(N2 + t, X[:, t, :])
                dense(KEY["mk0"] + t)
                if t:
                    norm_lo(N2 + t - 1, alo, ahi, t - 1)
            norm_lo(N2 + NT - 1, alo, ahi, NT - 1)
            for n in range(KEY["mv0"], KEY["xo0"]):
                dense(n)
            attention(PX)
            v.memset(tok[:, 0, :], 0.0).then_inc(zero_done, 1)
            for n in range(KEY["xo0"], ND - 1):
                dense(n)
            dve.wait_ge(gain_full, 64)
            evacuate(ND - 1, (0, 1))
            for t in range(NT):
                norm(N3 + t, X[:, t, :])
                if t + 2 < NT:
                    evacuate(ND - 1, (t + 2,))
                if t:
                    norm_lo(N3 + t - 1, alo, ahi, t - 1)
            norm_lo(N3 + NT - 1, alo, ahi, NT - 1)
            R = work[:, 0:2048]

            def r3(at, c, t=NT):
                return R[:, at:at + t * c].rearrange("p (t c) -> p t c", t=t)

            split_after(ND - 2)
            split_after(ND - 1)
            L = r3(0, ROUT_W)
            dve.wait_ge(route_mm, 1)
            v.tensor_copy(rT, ps[3][0:ROUT_W, :]).then_inc(rT_done, 1)
            dve.wait_ge(logits_done, 1)
            link(v.tensor_tensor(L, ps[0][:, 0:NT * ROUT_W].rearrange("p (t c) -> p t c", t=NT),
                                 rbias[:, :].unsqueeze(1).to_broadcast([P, NT, ROUT_W]), ALU.add))
            Lc, Lf = L[:, :, 0:NGRP], L[:, :, NGRP:]
            sh, ex, cm = r3(80, 4), r3(96, 4), r3(112, 1)
            link(v.tensor_reduce(R[:, 112:116], Lc, AX.X, ALU.max))
            bc4 = [P, NT, 4]
            v.tensor_tensor(sh, Lc, cm.to_broadcast(bc4), ALU.subtract).then_inc(r_step, 1)

            def first_max(src, at, top):
                e, m, o = r3(at, 4), r3(at + 16, 1), r3(at + 20, 4)
                link(v.tensor_tensor(e, src, top.to_broadcast(bc4), ALU.is_equal))
                link(v.tensor_tensor(e, e, tiew[:, :].unsqueeze(1).to_broadcast(bc4), ALU.mult))
                link(v.tensor_reduce(R[:, at + 16:at + 20], e, AX.X, ALU.max))
                link(v.tensor_tensor(o, e, m.to_broadcast(bc4), ALU.is_equal))
                return o

            og = first_max(Lc, 120, cm)
            fm = R[:, 160:224].rearrange("p (t g e) -> p t g e", t=NT, g=NGRP)
            link(v.tensor_tensor(fm, Lf.rearrange("p t (g e) -> p t g e", g=NGRP),
                                 og.unsqueeze(3).to_broadcast([P, NT, NGRP, PER]), ALU.mult))
            f4 = r3(224, 4)
            link(v.tensor_reduce(f4, fm.rearrange("p t g e -> p t e g"), AX.X, ALU.add))
            m1 = r3(240, 1)
            link(v.tensor_reduce(R[:, 240:244], f4, AX.X, ALU.max))
            o1 = first_max(f4, 244, m1)
            f4b = r3(288, 4)
            link(v.scalar_tensor_tensor(f4b, o1, -1e30, f4, ALU.mult, ALU.add))
            m2 = r3(304, 1)
            link(v.tensor_reduce(R[:, 304:308], f4b, AX.X, ALU.max))
            o2 = first_max(f4b, 308, m2)
            v.tensor_tensor(R[:, 388:392], R[:, 304:308], R[:, 240:244], ALU.subtract).then_inc(r_step, 1)
            oh = [R[:, 400 + 64 * b:464 + 64 * b].rearrange("p (t g e) -> p t g e", t=NT, g=NGRP) for b in range(2)]
            for o, ok in zip(oh, (o1, o2)):
                link(v.tensor_tensor(o, og.unsqueeze(3).to_broadcast([P, NT, NGRP, PER]),
                                     ok.unsqueeze(2).to_broadcast([P, NT, NGRP, PER]), ALU.mult))
            ohb = work[:, 2048:2080].bitcast(BF16)
            v.tensor_tensor(ohb, R[:, 400:464], R[:, 464:528], ALU.add).then_inc(onehot_done, 1)
            dve.wait_ge(r_exp, 2)
            link(v.tensor_reduce(R[:, 540:544], ex, AX.X, ALU.add))
            link(v.tensor_scalar(R[:, 544:548], R[:, 392:396], 1.0, None, ALU.add))
            link(v.tensor_tensor(R[:, 540:544], R[:, 540:544], R[:, 544:548], ALU.mult))
            link(v.reciprocal(R[:, 548:552], R[:, 540:544]))
            link(v.tensor_tensor(R[:, 552:556], R[:, 548:552], R[:, 392:396], ALU.mult))
            dve.wait_ge(rank_mm, 2)
            cnt = R[:, 560:576]
            nov = [R[:, 576 + 16 * b:592 + 16 * b] for b in range(2)]
            link(v.tensor_copy(cnt, ps[2][:, 0:NEXP]))
            link(v.tensor_scalar(nov[0], cnt, float(CHUNK), None, ALU.is_gt))
            for c in range(2, -(-T // CHUNK)):
                link(v.scalar_tensor_tensor(nov[0], cnt, float(CHUNK * c), nov[0], ALU.is_gt, ALU.add))
            link(v.tensor_copy(R[:, 620:636], nov[0]))
            cur = 0
            for s in (1, 2, 4, 8):
                link(v.tensor_copy(nov[1 - cur][:, 0:s], nov[cur][:, 0:s]))
                link(v.tensor_tensor(nov[1 - cur][:, s:], nov[cur][:, s:], nov[cur][:, 0:NEXP - s], ALU.add))
                cur = 1 - cur
            inc = nov[cur]
            exc = nov[1 - cur]
            link(v.tensor_tensor(exc, inc, R[:, 620:636], ALU.subtract))
            jump = R[:, 660:676]
            link(v.tensor_scalar(jump, exc, float(CHUNK), float(CHUNK * (NEXP - 1)), ALU.mult, ALU.add))
            link(v.scalar_tensor_tensor(jump, eiota, -float(CHUNK), jump, ALU.mult, ALU.add))
            rank = R[:, 900:964].rearrange("p (t e) -> p t e", t=NT)
            slot = R[:, 964:1028].rearrange("p (t e) -> p t e", t=NT)
            tmp = R[:, 1028:1092].rearrange("p (t e) -> p t e", t=NT)
            link(v.tensor_copy(rank, ps[1][:, 0:NT * NEXP].rearrange("p (t e) -> p t e", t=NT)))
            link(v.tensor_scalar(tmp, rank, float(CHUNK), None, ALU.is_ge))
            b16 = [P, NT, NEXP]
            link(v.tensor_tensor(tmp, tmp, jump.unsqueeze(1).to_broadcast(b16), ALU.mult))
            link(v.tensor_tensor(slot, rank, tmp, ALU.add))
            link(v.scalar_tensor_tensor(slot, eiota.unsqueeze(1).to_broadcast(b16), float(CHUNK), slot,
                                        ALU.mult, ALU.add))
            for b in range(2):
                link(v.tensor_tensor(tmp, slot, R[:, 400 + 64 * b:464 + 64 * b].rearrange("p (t e) -> p t e", t=NT),
                                     ALU.mult))
                link(v.tensor_reduce(R[:, 1100 + 4 * b:1104 + 4 * b], tmp, AX.X, ALU.add))
            NC = 2 * NT
            ge = tok[:, 1, 0:NC * (NLIST + 1)].rearrange("p (m c) -> p m c", m=NC)
            B = tok[:, 1, 256:256 + NC * 3 * NLIST].rearrange("p (m b c) -> p m b c", m=NC, b=3)
            at_slot = work[:, 1112:1112 + NC * CHUNK].rearrange("p (m s) -> p m s", m=NC)
            pos = R[:, 1100:1108]
            link(v.tensor_tensor(ge, pos.unsqueeze(2).to_broadcast([P, NC, NLIST + 1]),
                                 cgrid.unsqueeze(1).to_broadcast([P, NC, NLIST + 1]), ALU.is_ge))
            link(v.tensor_tensor(B[:, :, 2, :], ge[:, :, 0:NLIST], ge[:, :, 1:NLIST + 1], ALU.subtract))
            link(v.tensor_reduce(R[:, 1092:1100], ge, AX.X, ALU.add))
            link(v.scalar_tensor_tensor(R[:, 1092:1100], R[:, 1092:1100], -float(CHUNK), pos, ALU.mult, ALU.add))
            link(v.tensor_scalar(R[:, 1092:1100], R[:, 1092:1100], float(CHUNK), None, ALU.add))
            bl = [P, NC, NLIST]
            for b in range(2):
                m = slice(NT * b, NT * (b + 1))
                v.tensor_tensor(B[:, m, 0, :], B[:, m, 2, :], tokid.unsqueeze(2).to_broadcast([P, NT, NLIST]),
                                ALU.mult).then_inc(hot_done, 1)
            v.tensor_tensor(B[:, :, 1, :], B[:, :, 2, :], R[:, 548:556].unsqueeze(2).to_broadcast(bl), ALU.mult)\
                .then_inc(hot_done, 1)
            v.tensor_tensor(at_slot, siota.unsqueeze(1).to_broadcast([P, NC, CHUNK]),
                            R[:, 1092:1100].unsqueeze(2).to_broadcast([P, NC, CHUNK]), ALU.is_equal).then_inc(hot_done, 1)
            NO = MAXCH - NEXP
            cmpb = R[:, 700:700 + NO * NEXP].rearrange("p (i e) -> p i e", e=NEXP)
            link(v.tensor_tensor(cmpb, inc.unsqueeze(1).to_broadcast([P, NO, NEXP]),
                                 hgrid[:, 0:NO].unsqueeze(2).to_broadcast([P, NO, NEXP]), ALU.is_le))
            link(v.tensor_reduce(R[:, 640:640 + NO], cmpb, AX.X, ALU.add))
            link(v.tensor_scalar(R[:, 640:640 + NO], R[:, 640:640 + NO], float(NEXP - 1), None, ALU.min))
            link(v.tensor_copy(etab[:, 0:NEXP], eiota))
            link(v.tensor_copy(etab[:, NEXP:MAXCH], R[:, 640:640 + NO]))
            v.tensor_scalar(etab[:, MAXCH:MAXCH + 1], inc[:, NEXP - 1:NEXP], float(NEXP - 2), None, ALU.add)\
                .then_inc(route_done, 1)
            dve.wait_ge(list_mm, 1)
            none, found = tok[0:CHUNK, 1, 0:NLIST], ps[3][0:CHUNK, :]
            link(v.tensor_scalar(none, found[:, 2 * NLIST:3 * NLIST], -1.0, 1.0, ALU.mult, ALU.add))
            v.scalar_tensor_tensor(ltok[0:CHUNK, :], none, dummy[0:CHUNK, :], found[:, 0:NLIST], ALU.mult, ALU.add).then_inc(list_done, 1)
            v.tensor_copy(lwt[0:CHUNK, :], found[:, NLIST:2 * NLIST]).then_inc(list_done, 1)

            v.memset(sg, 0.0).then_inc(he_done, 1)
            dve.wait_ge(he_done, 1)

            def xg_lo_out(n):
                for b in range(2):
                    dve.wait_ge(xg_hi, n + b + 1)
                    v.tensor_tensor(xglo[:, 4 * b:4 * b + 4, :], ps[2 + b][:, 0:4 * CHUNK].rearrange("p (k t) -> p k t", k=4),
                                    xghi[:, 4 * b:4 * b + 4, :].bitcast(F32), ALU.subtract).then_inc(xg_lo, 1)

            def gated(n_silu, n_used, n_tp=None):
                dve.wait_ge(silu_done, n_silu)
                dve.wait_ge(used, n_used)
                if n_tp is not None:
                    dve.wait_ge(he_tp, n_tp)
                v.tensor_tensor(he, sg, ps[1][0:CHUNK, :], ALU.mult).then_inc(he_done, 1)

            def he_lo_out(n):
                dve.wait_ge(he_hi, n)
                v.tensor_tensor(helo, ps[6][:, 0:KF * CHUNK].rearrange("p (k t) -> p k t", k=KF), hehi.bitcast(F32),
                                ALU.subtract).then_inc(he_lo, 1)

            split_expert(2)
            xg_lo_out(0)
            split_expert(3)
            split_expert(4)
            split_expert(5)
            split_expert(6)
            gated(1, 4)
            xg_lo_out(2)
            he_lo_out(1)
            dve.wait_ge(route_done, 1)
            turns = dve.value_load(etab[0:1, MAXCH:MAXCH + 1], min_val=NEXP - 2, max_val=MAXCH - 3)

            def turn(j, last):
                for m in (7, 8, 9, 10):
                    split_expert(m, j)
                gated(j + 1, 6 * (j - 1) + 8, j)
                xg_lo_out(2 * j + 2)
                split_expert(11, j)
                if not last:
                    split_expert(12, j)
                he_lo_out(j + 1)

            with dve.Fori(1, turns + 1) as j:
                turn(j, False)
            turn(turns + 1, True)
            dve.wait_ge(gain_full, 80)
            for t in range(NT):
                norm(N4 + t, X[:, t, :], tok[:, t, :])

        @block.tensor
        def _(pe):
            mm = nc.tensor.matmul

            def three(out_, ahi_, alo_, bhi_, blo_, first, last):
                mm(out_, ahi_, bhi_, start=first, stop=False)
                mm(out_, ahi_, blo_, start=False, stop=False)
                return mm(out_, alo_, bhi_, start=False, stop=last)

            def dense(n):
                pe.wait_ge(lo_done, n + 1)
                hi = whi[:, n % SPLIT, :].rearrange("p (k n) -> p k n", k=KD)
                lo = wlo[:, n % SPLIT, :].rearrange("p (k n) -> p k n", k=KD)
                mem = ORDER[n][:2] in ("mk", "mv")
                xh, xl, nt = (memhi, memlo, MEM) if mem else (ahi, alo, T)
                for g in of_piece[n]:
                    _, kind, idx, c0, w, eng = groups[g]
                    if kind == "C":
                        kv, b = idx // 2, idx % 2
                        pe.wait_ge(flo_done, kv + 1)
                        for j in range(8):
                            ins = three(ps[6 + kv][0:2 * N_CMP, 0:CMP_HID], fhi[kv][:, 8 * b + j, :],
                                        flo[kv][:, 8 * b + j, :], hi[:, j, :], lo[:, j, :],
                                        b == 0 and j == 0, b == 1 and j == 7)
                        ins.then_inc(grp_done, 1)
                        continue
                    if g >= DRING and groups[g - DRING][5]:
                        e = groups[g - DRING][5]
                        pe.wait_ge(evac[e], evacs(g - DRING, e))
                    bank = ps[g % DRING]
                    if ORDER[n] in ("out0", "xo0"):
                        pe.wait_ge((PA if ORDER[n] == "out0" else PX).ot_lo, 2 * (idx + 1))
                    for k in range(KD):
                        if kind == "F":
                            wc = slice(c0, c0 + P)
                            ins = three(bank[:, 0:nt], hi[:, k, wc], lo[:, k, wc], xh[:, k, :], xl[:, k, :],
                                        k == 0, k == KD - 1)
                        else:
                            tc = slice(idx * P, (idx + 1) * P)
                            ins = three(bank[:, 0:w], xh[:, k, tc], xl[:, k, tc], hi[:, k, c0:c0 + w],
                                        lo[:, k, c0:c0 + w], k == 0, k == KD - 1)
                    ins.then_inc(grp_done, 1)

            def norm_transposes(q):
                pe.wait_ge(h_done, q + 1)
                if q >= 2:
                    pe.wait_ge(ntp_lo, 2 * (q - 1))
                for b in range(2):
                    for m in range(4):
                        c = (4 * b + m) * P
                        ins = nc.tensor.transpose(ps[4 + 2 * (q % 2) + b][:, m * P:(m + 1) * P],
                                                  tok[:, 2 + q % 2, c:c + P], ident[:, :])
                    ins.then_inc(ntp_done, 1)

            pe.wait_ge(ident_in, 16)
            for t in range(NT):
                norm_transposes(NX + t)
            pe.wait_ge(ntp_lo, 2 * NT)
            dense(0)
            def narrow(bank, w_hi, w_lo, n):
                for k in range(KD):
                    ins = three(bank[0:n, 0:T], w_hi[:, k, :], w_lo[:, k, :], ahi[:, k, :], alo[:, k, :],
                                k == 0, k == KD - 1)
                return ins

            def to_tokens(bank, src, n):
                for t in range(NT):
                    ins = nc.tensor.transpose(bank[:, t * n:(t + 1) * n], src[:, t * P:(t + 1) * P], ident[0:n, 0:n])
                return ins

            pe.wait_ge(sm_lo, 1)
            narrow(ps[5], wsm_hi, wsm_lo, SMALL_W).then_inc(smallT_mm, 1)
            dense(1)
            pe.wait_ge(zT_done, 1)
            to_tokens(ps[4], zT, SMALL_W).then_inc(small_mm, 1)
            dense(2)
            pe.wait_ge(lf_done, 1)
            pe.wait_ge(const_in, 16 * N_CONST)
            for t in range(NT):
                ins = mm(ps[5][0:FOX_H, t * P:T], zz[:, 4, t, 0:FOX_H], tri[:, 0:T - t * P],
                         start=(t == 0), stop=(t == NT - 1))
            ins.then_inc(cum_mm, 1)
            for n in range(3, KEY["out0"]):
                dense(n)
                if ORDER[n] == "nq1":
                    pe.wait_ge(gelu_done, 2)
                    for m in range(4):
                        w = 2 * N_CMP
                        ins = nc.tensor.transpose(ps[6][:, w * m:w * (m + 1)],
                                                  gtok[:, m // 2, P * (m % 2):P * (m % 2 + 1)], ident[0:w, 0:w])
                    ins.then_inc(gT_mm, 1)
                if ORDER[n] == "fv0":
                    pe.wait_ge(gT_done, 1)
                    pe.wait_ge(const2_in, 16 * N_CONST2)
                    for hb in range(2):
                        ins = mm(ps[4][0:DH, 0:2 * N_CMP], w2[:, 0, hb, :], gT[:, 0, hb, :],
                                 start=(hb == 0), stop=(hb == 1))
                    ins.then_inc(kv2_mm, 1)
                    for g in range(NSA_G):
                        for hb in range(2):
                            ins = mm(ps[5][0:N_CMP, DH * g:DH * (g + 1)], gT[:, 1, hb, N_CMP * g:N_CMP * (g + 1)],
                                     w2[:, 1, hb, :], start=(hb == 0), stop=(hb == 1))
                    ins.then_inc(kv2_mm, 1)
                if ORDER[n] == "fv1":
                    pe.wait_ge(kc_done, 1)
                    pe.wait_ge(bf_done, 1)
                    pe.wait_ge(rows_in, 16 * 6)
                    for b in range(2):
                        w = NSA_R * CMP_PAD
                        mm(ps[6 + b][:, 0:NT * w].rearrange("p (i r c) -> p i r c", i=NT, r=NSA_R), identb,
                           maskc.rearrange("p (i c) -> p i c", i=NT).unsqueeze(2).to_broadcast([P, NT, NSA_R, CMP_PAD]),
                           start=True, stop=False)
                        for r in range(NSA_R):
                            for i in range(NT):
                                c0 = w * i + CMP_PAD * r
                                ins = mm(ps[6 + b][:, c0:c0 + CMP_PAD], Qn[0:P, NSA_R * b + r, i * P:(i + 1) * P],
                                         Kc[0:P, b, :], start=False, stop=(r == NSA_R - 1 and i == NT - 1))
                        ins.then_inc(cs_done, 1)
            pe.wait_ge(vc_done, 1)
            pe.wait_ge(csub_done, 2)
            pe.wait_ge(pooled_done, 2)
            for f in range(2):
                mm(ps[6 + f][:, :], wpool[:, f, :], pooled[:, f, :], start=True, stop=True).then_inc(mix_mm, 1)

            def attention(ph):
                for k in range(ph.steps):
                    if ph.score(k):
                        i, kind, h, nb = ph.units[k]
                        s = ph.sidx[k]
                        bank = ps[s % 3]
                        if s >= 3:
                            pe.wait_ge(ph.exp_done, s - 2)
                        qc = slice(i * P, (i + 1) * P)
                        if kind == "x":
                            for e in range(2):
                                ins = mm(bank[:, 0:MEM], QTx[:, 2 * h + e, qc], KTm[:, 2 * h + e, :],
                                         start=(e == 0), stop=(e == 1))
                        else:
                            q = (Qf if kind == "f" else Qn)[0:P, h, qc]
                            kk = {"f": Kf, "s": Ks, "w": Kw}[kind][0:P, h if kind == "f" else h // NSA_R, 0:P * nb]
                            mm(bank[:, 0:P * nb], q, kk, start=True, stop=False)
                            ins = mm(bank[:, P * i:P * nb], identb, maskb, start=False, stop=True)
                        ins.then_inc(ph.scores_done, 1)
                    u = k - LAG_T
                    if ph.has(u):
                        i, kind, h, nb = ph.units[u]
                        bank = ps[3 + u % 2]
                        if u >= 2:
                            pe.wait_ge(ph.pt_done, u - 1)
                        if kind == "c":
                            ins = nc.tensor.transpose(bank[0:NSA_R * CMP_PAD, 0:P],
                                                      Pc[:, i, NSA_R * h:NSA_R * (h + 1), :].rearrange("p r c -> p (r c)"),
                                                      ident[:, :])
                        else:
                            s = ph.sidx[u]
                            pe.wait_ge(ph.exp_done, s + 1)
                            for b in range(nb):
                                ins = nc.tensor.transpose(bank[:, P * b:P * (b + 1)], Pr[s % len(Pr)][:, P * b:P * (b + 1)],
                                                          ident[:, :])
                        ins.then_inc(ph.tp_done, 1)
                    u = k - LAG_V
                    if ph.has(u):
                        i, kind, h, nb = ph.units[u]
                        bank = ps[5 + u % 2]
                        pt = PTr[u % len(PTr)]
                        pe.wait_ge(ph.pt_done, u + 1)
                        if ph is PA and u == 0:
                            pe.wait_ge(mix_lo, 2)
                        if u >= 2:
                            pe.wait_ge(ph.o_done, u - 1)
                        if kind == "c":
                            rws = NSA_R * CMP_PAD
                            ins = mm(bank[:, 0:NSA_R * DH], pt[0:rws, 0:P], Vc[0:rws, h, :], start=True, stop=True)
                        else:
                            w = D // MEM_H if kind == "x" else DH
                            for b in range(nb):
                                if kind == "x":
                                    val = Vm[:, b, w * h:w * (h + 1)]
                                elif kind == "f":
                                    val = Vf[:, b, w * h:w * (h + 1)]
                                else:
                                    val = (Vs if kind == "s" else Vw)[:, b, DH * (h // NSA_R):DH * (h // NSA_R) + DH]
                                ins = mm(bank[:, 0:w], pt[:, P * b:P * (b + 1)], val, start=(b == 0), stop=(b == nb - 1))
                        ins.then_inc(ph.pv_done, 1)
                    for r, i, fb in ph.rounds(k):
                        pe.wait_ge(ph.o_done, ph.per * (i + 1))
                        if 0 < r < 2 * NT - 1:
                            pe.wait_ge(ph.ot_lo, r)
                        for m, f in enumerate(fb):
                            ins = nc.tensor.transpose(ph.ot_bank(r)[:, m * P:(m + 1) * P],
                                                      tok[:, 2 + i % 2, f * P:(f + 1) * P], ident[:, :])
                        ins.then_inc(ph.ot_done, 1)

            pe.wait_ge(evac["act"], evacs(of_piece[KEY["out0"]][0] - 1, "act"))
            pe.wait_ge(evac["dve"], evacs(of_piece[KEY["out0"]][0] - 1, "dve"))
            pe.wait_ge(pc_done, 1)
            pe.wait_ge(cumrow_in, 32)
            attention(PA)
            dense(KEY["out0"])
            dense(KEY["out1"])
            for t in range(MT):
                norm_transposes(NM + t)
            dense(KEY["out2"])
            dense(KEY["out3"])
            pe.wait_ge(ntp_lo, 2 * (NM + MT))
            for t in range(NT):
                dense(KEY["mk0"] + t)
                norm_transposes(N2 + t)
            for n in range(KEY["mv0"], KEY["xo0"]):
                if ORDER[n] == "xq0":
                    pe.wait_ge(ntp_lo, 2 * N3)
                dense(n)
            pe.wait_ge(evac["act"], evacs(of_piece[KEY["xo0"]][0] - 1, "act"))
            attention(PX)
            for n in range(KEY["xo0"], ND):
                dense(n)
            for t in range(NT):
                norm_transposes(N3 + t)
            pe.wait_ge(ntp_lo, 2 * N4)
            pe.wait_ge(sm_lo, 2)
            pe.wait_ge(evac["dve"], evacs(len(groups) - 1, "dve"))
            narrow(ps[3], wrt_hi, wrt_lo, ROUT_W).then_inc(route_mm, 1)
            pe.wait_ge(rT_done, 1)
            to_tokens(ps[0], rT, ROUT_W).then_inc(logits_done, 1)
            pe.wait_ge(onehot_done, 1)
            ohb = work[:, 2048:2080].bitcast(BF16).rearrange("p (t e) -> p t e", t=NT)
            for t in range(NT):
                for s in range(t + 1):
                    ins = mm(ps[1][:, NEXP * t:NEXP * (t + 1)], ones if s < t else sut, ohb[:, s, :],
                             start=(s == 0), stop=(s == t))
            ins.then_inc(rank_mm, 1)
            for s in range(NT):
                ins = mm(ps[2][:, 0:NEXP], ones, ohb[:, s, :], start=(s == 0), stop=(s == NT - 1))
            ins.then_inc(rank_mm, 1)
            pe.wait_ge(hot_done, 4)
            B = tok[:, 1, 256:256 + 2 * NT * 3 * NLIST].rearrange("p (m b) -> p m b", m=2 * NT)
            at_slot = work[:, 1112:1112 + 2 * NT * CHUNK].rearrange("p (m s) -> p m s", m=2 * NT)
            for m in range(2 * NT):
                ins = mm(ps[3][0:CHUNK, 0:3 * NLIST], at_slot[:, m, :], B[:, m, :], start=(m == 0), stop=(m == 2 * NT - 1))
            ins.then_inc(list_mm, 1)
            pe.wait_ge(route_done, 1)

            def in_piece(bank, m, half_):
                hi, lo = (x.rearrange("p (k f) -> p k f", k=KF) for x in moe_split(m))
                for k in range(KF):
                    kk = KF * half_ + k
                    ins = three(bank[0:CHUNK, :], xghi[:, kk, :], xglo[:, kk, :], hi[:, k, :], lo[:, k, :],
                                kk == 0, kk == KD - 1)
                ins.then_inc(used, 1)

            def down_piece(bank, m):
                hi, lo = (x.rearrange("p (k f) -> p k f", k=KF) for x in moe_split(m))
                for k in range(KF):
                    ins = three(bank[0:CHUNK, :], hehi[:, k, :], helo[:, k, :], hi[:, k, :], lo[:, k, :],
                                k == 0, k == KF - 1)
                ins.then_inc(used, 1)

            def xg_transposes():
                for b in range(2):
                    for m in range(4):
                        c = (4 * b + m) * P
                        ins = nc.tensor.transpose(ps[2 + b][:, m * CHUNK:(m + 1) * CHUNK], tok[0:CHUNK, 0, c:c + P],
                                                  ident[0:CHUNK, 0:CHUNK])
                    ins.then_inc(xg_tp, 1)

            def he_transposes():
                for m in range(KF):
                    ins = nc.tensor.transpose(ps[6][:, m * CHUNK:(m + 1) * CHUNK], he[:, m * P:(m + 1) * P],
                                              ident[0:CHUNK, 0:CHUNK])
                ins.then_inc(he_tp, 1)

            pe.wait_ge(xg_in, 16)
            xg_transposes()
            pe.wait_ge(xg_lo, 2)
            for m in range(4):
                pe.wait_ge(lo_done, ND + m + 1)
                in_piece(ps[m // 2], m, m % 2)
            pe.wait_ge(xg_in, 32)
            xg_transposes()
            pe.wait_ge(he_done, 2)
            he_transposes()
            turns = pe.value_load(etab[0:1, MAXCH:MAXCH + 1], min_val=NEXP - 2, max_val=MAXCH - 3)
            with pe.Fori(1, turns + 2) as j:
                n0 = 6 * (j - 1) + (NMP + 1)
                pe.wait_ge(xg_lo, 2 * j + 2)
                pe.wait_ge(silu_done, j)
                for m in range(2):
                    pe.wait_ge(lo_done, n0 + m)
                    in_piece(ps[0], 4 + m, m)
                pe.wait_ge(he_done, j + 1)
                for m in range(2):
                    pe.wait_ge(lo_done, n0 + 2 + m)
                    in_piece(ps[1], 6 + m, m)
                pe.wait_ge(xg_in, 16 * j + 32)
                xg_transposes()
                pe.wait_ge(he_lo, j)
                for m in range(2):
                    pe.wait_ge(lo_done, n0 + 4 + m)
                    down_piece(ps[4 + m], 8 + m)
                pe.wait_ge(he_done, j + 2)
                he_transposes()
            pe.wait_ge(he_lo, turns + 2)
            for m in range(2):
                pe.wait_ge(lo_done, 6 * turns + (NMP + 7 + m))
                down_piece(ps[4 + m], 10 + m)


_INS = ["x", "mem", "mix_norm_g", "w_in", "fox_forget_b", "pool_w", "cmp_w1_k", "cmp_w2_k", "cmp_w1_v",
        "cmp_w2_v", "nsa_gate_b", "w_out", "xattn_norm_g", "mem_norm_g", "xattn_wq", "xattn_wk", "xattn_wv",
        "xattn_wo", "ffn_norm_g", "router_coarse_w", "router_coarse_b", "router_fine_w", "router_fine_b",
        "exp_w_gate", "exp_w_up", "exp_w_down", "final_norm_g"]


def constants():
    import numpy as np
    f = np.float32
    i = np.arange(P)
    neg = f(-1e30)
    c_end = np.arange(CMP_PAD) * CMP_STRIDE + CMP_LEN - 1
    tok_ = np.arange(NT)[None, :] * P + i[:, None]
    maskc = np.where(tok_[:, :, None] >= c_end[None, None, :], f(0), neg)
    bf = np.concatenate([np.eye(P), np.where(i[None, :] <= i[:, None], 0, neg), maskc.reshape(P, -1),
                         i[:, None] < i[None, :], np.ones((P, P))], axis=1).astype(f)
    pool = np.zeros((P, 2, 17), f)
    for g, w in enumerate(POOL_WINDOWS):
        r = slice(64 * (g % 2), 64 * (g % 2) + 64)
        pool[r, g // 2, 0] = 1.0 / w
        pool[r, g // 2, 1:17] = w / np.minimum(np.arange(16) + 1, w)
    slopes = np.exp2(f(-8.0) * np.arange(1, NSA_H + 1, dtype=f) / f(NSA_H)).astype(f)
    t = np.arange(T, dtype=f)
    qrows = np.stack([-slopes[:, None] * t[None, :], np.repeat(slopes[:, None], T, 1)]).astype(f)
    krows = np.stack([np.ones((NSA_G, T)), np.repeat(t[None], NSA_G, 0)]).astype(f)
    crows = np.stack([np.ones((NSA_G, CMP_PAD)), np.repeat(c_end[None], NSA_G, 0)]).astype(f)
    row = np.concatenate([np.arange(MAXCH), [4, 3, 2, 1], np.arange(NEXP)]).astype(f)
    tabs = np.concatenate([np.repeat(row[None], P, 0), tok_, np.repeat(CHUNK * np.arange(NLIST + 1)[None], P, 0),
                           T + i[:, None], np.repeat(i[None, :CHUNK], P, 0)], axis=1).astype(f)
    return {"ident": np.eye(P, dtype=f), "tri": (np.arange(T)[None, :] >= i[:, None]).astype(f), "bf": bf,
            "pool": pool, "tabs": tabs, "qrows": qrows, "krows": krows, "crows": crows,
            "ones": np.ones((1, FOX_H, T), f)}


def kernel(**inputs):
    import numpy as _np
    import concourse.bacc as _bacc
    from concourse.bass_utils import run_bass_kernel_spmd as _run

    nc = _bacc.Bacc("TRN2", target_bir_lowering=False, num_devices=1)
    arrays = {}

    def give(name, a):
        a = _np.ascontiguousarray(a)
        arrays[name] = a
        return nc.dram_tensor(name, a.shape, mybir.dt.from_np(a.dtype), kind="ExternalInput").ap()

    A = {n: give(f"in_{n}", _np.asarray(inputs[n])) for n in _INS}
    for c in "kv":
        pe = _np.asarray(inputs[f"cmp_pe_{c}"])[0].reshape(16, 2, DH).transpose(1, 2, 0).reshape(P, 16)
        A[f"pe_{c}"] = give(f"in_pe_{c}", pe)
    A["pscale"] = give("in_pscale", _np.asarray(inputs["pool_scale"])[0].reshape(2, P).T)
    C = {n: give(f"c_{n}", a) for n, a in constants().items()}
    out = nc.dram_tensor("out_0", (1, T, D), F32, kind="ExternalOutput").ap()
    build(nc, A, C, out)
    r = _run(nc, [arrays], core_ids=[0])
    return r.results[0]["out_0"]
```
